# Optimizing a Trainium2 kernel written in Bass

```python
import jax, jax.numpy as jnp
from jax import lax
import numpy as np
import math

D_MODEL = 1024
BATCH = 1
SEQ = 512
DEPTH = 2

N_A_LAYERS = DEPTH // 2
N_B_LAYERS = DEPTH - N_A_LAYERS
HEAD_DIM = 64
SB_HEADS = D_MODEL // HEAD_DIM
NSA_HEADS = D_MODEL // HEAD_DIM
NSA_KV_GROUPS = 4
NSA_HPG = NSA_HEADS // NSA_KV_GROUPS
CMP_LEN = 32
CMP_STRIDE = 16
CMP_HIDDEN = 256
SEL_LEN = 64
SEL_TOPK = 16
WINDOW = 512
D_FF = 4 * D_MODEL
ROPE_THETA = 500000.0
ROT_DIM = HEAD_DIM // 4
Q_BLOCK = 128
NORM_EPS = 1e-5
NEG = -1e30
FORCED_SCORE = 1e6


def rms_norm(x, g):
    xf = x.astype(jnp.float32)
    y = xf * lax.rsqrt(jnp.mean(xf * xf, axis=-1, keepdims=True) + NORM_EPS)
    return (y * g.astype(jnp.float32)).astype(x.dtype)

def partial_rope(x):
    s = x.shape[1]
    half = ROT_DIM // 2
    inv_freq = ROPE_THETA ** (-jnp.arange(half, dtype=jnp.float32) * 2.0 / ROT_DIM)
    ang = jnp.arange(s, dtype=jnp.float32)[:, None] * inv_freq[None, :]
    cos = jnp.cos(ang)[None, :, None, :]
    sin = jnp.sin(ang)[None, :, None, :]
    xr = x[..., :ROT_DIM].astype(jnp.float32)
    x1, x2 = xr[..., :half], xr[..., half:]
    rot = jnp.concatenate([x1 * cos - x2 * sin, x2 * cos + x1 * sin], axis=-1).astype(x.dtype)
    return jnp.concatenate([rot, x[..., ROT_DIM:]], axis=-1)

def to_qblocks(a):
    b, s = a.shape[0], a.shape[1]
    return jnp.moveaxis(a.reshape((b, s // Q_BLOCK, Q_BLOCK) + a.shape[2:]), 1, 0)

def from_qblocks(a):
    a = jnp.moveaxis(a, 0, 1)
    return a.reshape((a.shape[0], a.shape[1] * a.shape[2]) + a.shape[3:])

def sqrelu_mlp(x, w1, w2):
    h = jax.nn.relu(x @ w1)
    return (h * h) @ w2

def stick_breaking_attention(h, w_qkv, w_o):
    b, s, _ = h.shape
    n_qb = s // Q_BLOCK
    qkv = (h @ w_qkv).reshape(b, s, 3, SB_HEADS, HEAD_DIM)
    q, k, v = qkv[:, :, 0], qkv[:, :, 1], qkv[:, :, 2]
    scale = HEAD_DIM ** -0.5
    key_pos = jnp.arange(s)

    def block(args):
        qi, q_blk = args
        t = qi * Q_BLOCK + jnp.arange(Q_BLOCK)
        z = jnp.einsum('bqhd,bshd->bhqs', q_blk, k).astype(jnp.float32) * scale
        causal = key_pos[None, :] < t[:, None]
        log_1m = jnp.where(causal, jax.nn.log_sigmoid(-z), 0.0)
        excl = lax.cumsum(log_1m, axis=3, reverse=True) - log_1m
        a = jnp.where(causal, jnp.exp(jax.nn.log_sigmoid(z) + excl), 0.0)
        return jnp.einsum('bhqs,bshd->bqhd', a.astype(v.dtype), v)

    o = lax.map(block, (jnp.arange(n_qb), to_qblocks(q)))
    return from_qblocks(o).reshape(b, s, SB_HEADS * HEAD_DIM) @ w_o

def nsa_shared_kv(h, kv_norm, w_kv, cmp_pos, cmp_w1, cmp_w2):
    b, s, _ = h.shape
    hn = rms_norm(h, kv_norm)
    kv = (hn @ w_kv).reshape(b, s, 3, 2, NSA_KV_GROUPS, HEAD_DIM)
    n_cmp = (s - CMP_LEN) // CMP_STRIDE + 1
    idx = jnp.arange(n_cmp)[:, None] * CMP_STRIDE + jnp.arange(CMP_LEN)[None, :]
    blk = kv[:, :, 0][:, idx]
    blk = blk + jnp.transpose(cmp_pos, (1, 0, 2))[None, None, :, :, None, :]
    blk = jnp.transpose(blk, (0, 1, 3, 4, 2, 5)).reshape(b, n_cmp, 2, NSA_KV_GROUPS, CMP_LEN * HEAD_DIM)
    hid = jax.nn.gelu(jnp.einsum('bncgf,cfe->bncge', blk, cmp_w1))
    cmp = jnp.einsum('bncge,ced->bncgd', hid, cmp_w2)
    k_cmp, v_cmp = cmp[:, :, 0], cmp[:, :, 1]
    k_slc, v_slc = partial_rope(kv[:, :, 1, 0]), kv[:, :, 1, 1]
    k_win, v_win = partial_rope(kv[:, :, 2, 0]), kv[:, :, 2, 1]
    return (k_cmp, v_cmp, k_slc, v_slc, k_win, v_win)

def nsa_attention(h, w_q, gate_b, w_o, shared):
    k_cmp, v_cmp, k_slc, v_slc, k_win, v_win = shared
    b, s, _ = h.shape
    G, HPG, DH = NSA_KV_GROUPS, NSA_HPG, HEAD_DIM
    n_cmp = k_cmp.shape[1]
    n_sel = s // SEL_LEN
    n_qb = s // Q_BLOCK
    topk = min(SEL_TOPK, n_sel)
    scale = DH ** -0.5

    proj = h @ w_q
    q = proj[..., :NSA_HEADS * DH].reshape(b, s, NSA_HEADS, DH)
    gates = jax.nn.sigmoid((proj[..., NSA_HEADS * DH:] + gate_b).astype(jnp.float32)).reshape(b, s, 3, NSA_HEADS)
    q_rot = partial_rope(q)

    cmp_start = jnp.arange(n_cmp) * CMP_STRIDE
    cmp_end = cmp_start + CMP_LEN - 1
    sel_ids = jnp.arange(n_sel)
    sel_start = sel_ids * SEL_LEN
    overlap = ((cmp_start[:, None] < sel_start[None, :] + SEL_LEN)
               & (cmp_start[:, None] + CMP_LEN > sel_start[None, :])).astype(jnp.float32)
    k_sel_blocks = jnp.transpose(k_slc.reshape(b, n_sel, SEL_LEN, G, DH), (0, 3, 1, 2, 4))
    v_sel_blocks = jnp.transpose(v_slc.reshape(b, n_sel, SEL_LEN, G, DH), (0, 3, 1, 2, 4))
    pad = ((0, 0), (WINDOW, 0), (0, 0), (0, 0))
    k_win_p = jnp.pad(k_win, pad)
    v_win_p = jnp.pad(v_win, pad)
    gather = jax.vmap(jax.vmap(lambda blocks, ids: blocks[ids]))

    def block(args):
        qi, q_blk, qr_blk = args
        q0 = qi * Q_BLOCK
        t = q0 + jnp.arange(Q_BLOCK)
        qg = q_blk.reshape(b, Q_BLOCK, G, HPG, DH)
        qrg = qr_blk.reshape(b, Q_BLOCK, G, HPG, DH)

        sc = jnp.einsum('bqghd,bngd->bghqn', qg, k_cmp).astype(jnp.float32) * scale
        valid_c = cmp_end[None, :] <= t[:, None]
        p_cmp = jax.nn.softmax(jnp.where(valid_c, sc, NEG), axis=-1)
        p_cmp = p_cmp * jnp.any(valid_c, axis=-1)[:, None]
        o_cmp = jnp.einsum('bghqn,bngd->bqghd', p_cmp.astype(v_cmp.dtype), v_cmp)

        imp = jnp.einsum('bghqn,nm->bgqm', p_cmp, overlap)
        blk_t = t // SEL_LEN
        forced = (sel_ids[None, :] == 0) | (sel_ids[None, :] == blk_t[:, None]) | (sel_ids[None, :] == blk_t[:, None] - 1)
        causal_b = sel_ids[None, :] <= blk_t[:, None]
        imp = jnp.where(causal_b, jnp.where(forced, FORCED_SCORE, imp), -jnp.inf)
        _, top_idx = lax.top_k(imp, topk)
        k_sel = gather(k_sel_blocks, top_idx)
        v_sel = gather(v_sel_blocks, top_idx)
        ss = jnp.einsum('bqghd,bgqkld->bghqkl', qrg, k_sel).astype(jnp.float32) * scale
        key_pos = top_idx[..., None] * SEL_LEN + jnp.arange(SEL_LEN)
        valid_s = key_pos <= t[None, None, :, None, None]
        ss = jnp.where(valid_s[:, :, None], ss, NEG)
        p_sel = jax.nn.softmax(ss.reshape(b, G, HPG, Q_BLOCK, topk * SEL_LEN), axis=-1).reshape(ss.shape)
        o_sel = jnp.einsum('bghqkl,bgqkld->bqghd', p_sel.astype(v_sel.dtype), v_sel)

        k_w = lax.dynamic_slice_in_dim(k_win_p, q0, WINDOW + Q_BLOCK, axis=1)
        v_w = lax.dynamic_slice_in_dim(v_win_p, q0, WINDOW + Q_BLOCK, axis=1)
        sw = jnp.einsum('bqghd,bsgd->bghqs', qrg, k_w).astype(jnp.float32) * scale
        kpos = q0 - WINDOW + jnp.arange(WINDOW + Q_BLOCK)
        diff = t[:, None] - kpos[None, :]
        valid_w = (diff >= 0) & (diff < WINDOW) & (kpos[None, :] >= 0)
        p_w = jax.nn.softmax(jnp.where(valid_w, sw, NEG), axis=-1)
        o_win = jnp.einsum('bghqs,bsgd->bqghd', p_w.astype(v_w.dtype), v_w)

        return jnp.stack([o_cmp, o_sel, o_win], axis=2).reshape(b, Q_BLOCK, 3, NSA_HEADS, DH)

    o = from_qblocks(lax.map(block, (jnp.arange(n_qb), to_qblocks(q), to_qblocks(q_rot))))
    out = jnp.einsum('bsch,bschd->bshd', gates.astype(o.dtype), o).reshape(b, s, NSA_HEADS * DH)
    return out @ w_o

def first_inputs(seed: int = 0) -> dict:
    key = jax.random.key(seed)
    ks = jax.random.split(key, 16)
    f32 = jnp.float32

    def w(k, shape, fan_in):
        return jax.random.normal(k, shape, f32) * fan_in ** -0.5

    x = jax.random.normal(ks[0], (BATCH, SEQ, D_MODEL), f32)
    norm_gain = 1.0 + 0.02 * jax.random.normal(ks[1], (DEPTH, 2, D_MODEL), f32)
    sb_w_qkv = w(ks[2], (N_A_LAYERS, D_MODEL, 3 * SB_HEADS * HEAD_DIM), D_MODEL)
    sb_w_o = w(ks[3], (N_A_LAYERS, SB_HEADS * HEAD_DIM, D_MODEL), SB_HEADS * HEAD_DIM)
    kv_norm = 1.0 + 0.02 * jax.random.normal(ks[4], (D_MODEL,), f32)
    nsa_w_kv = w(ks[5], (D_MODEL, 3 * 2 * NSA_KV_GROUPS * HEAD_DIM), D_MODEL)
    cmp_pos = 0.1 * jax.random.normal(ks[6], (2, CMP_LEN, HEAD_DIM), f32)
    cmp_w1 = w(ks[7], (2, CMP_LEN * HEAD_DIM, CMP_HIDDEN), CMP_LEN * HEAD_DIM)
    cmp_w2 = w(ks[8], (2, CMP_HIDDEN, HEAD_DIM), CMP_HIDDEN)
    nsa_w_q = w(ks[9], (N_B_LAYERS, D_MODEL, NSA_HEADS * HEAD_DIM + 3 * NSA_HEADS), D_MODEL)
    nsa_gate_b = 0.1 * jax.random.normal(ks[10], (N_B_LAYERS, 3 * NSA_HEADS), f32)
    nsa_w_o = w(ks[11], (N_B_LAYERS, NSA_HEADS * HEAD_DIM, D_MODEL), NSA_HEADS * HEAD_DIM)
    mlp_w1 = w(ks[12], (DEPTH, D_MODEL, D_FF), D_MODEL)
    mlp_w2 = w(ks[13], (DEPTH, D_FF, D_MODEL), D_FF)
    final_norm = 1.0 + 0.02 * jax.random.normal(ks[14], (D_MODEL,), f32)
    return {"x": x, "norm_gain": norm_gain, "sb_w_qkv": sb_w_qkv, "sb_w_o": sb_w_o,
            "kv_norm": kv_norm, "nsa_w_kv": nsa_w_kv, "cmp_pos": cmp_pos, "cmp_w1": cmp_w1,
            "cmp_w2": cmp_w2, "nsa_w_q": nsa_w_q, "nsa_gate_b": nsa_gate_b, "nsa_w_o": nsa_w_o,
            "mlp_w1": mlp_w1, "mlp_w2": mlp_w2, "final_norm": final_norm}

def first_block(x, norm_gain, sb_w_qkv, sb_w_o, kv_norm, nsa_w_kv, cmp_pos, cmp_w1, cmp_w2,
              nsa_w_q, nsa_gate_b, nsa_w_o, mlp_w1, mlp_w2, final_norm):
    h = x
    shared = None
    for layer in range(DEPTH):
        hn = rms_norm(h, norm_gain[layer, 0])
        if layer < N_A_LAYERS:
            h = h + stick_breaking_attention(hn, sb_w_qkv[layer], sb_w_o[layer])
        else:
            j = layer - N_A_LAYERS
            h = h + nsa_attention(hn, nsa_w_q[j], nsa_gate_b[j], nsa_w_o[j], shared)
        h = h + sqrelu_mlp(rms_norm(h, norm_gain[layer, 1]), mlp_w1[layer], mlp_w2[layer])
        if layer == N_A_LAYERS - 1:
            shared = nsa_shared_kv(h, kv_norm, nsa_w_kv, cmp_pos, cmp_w1, cmp_w2)
    return rms_norm(h, final_norm)


DEPTH_2 = 1

MIX_WIDTH = D_MODEL
SWA_Q_HEADS = 8
SWA_KV_HEADS = 2
SWA_GROUP = SWA_Q_HEADS // SWA_KV_HEADS
WINDOW_2 = 128
BLOCK = 128
DIFF_HEADS = 4
DIFF_VDIM = 2 * HEAD_DIM
SWA_Q_COLS = SWA_Q_HEADS * HEAD_DIM
SWA_KV_COLS = SWA_KV_HEADS * HEAD_DIM
DIFF_QK_COLS = DIFF_HEADS * 2 * HEAD_DIM
DIFF_V_COLS = DIFF_HEADS * DIFF_VDIM
IN_COLS = SWA_Q_COLS + 2 * SWA_KV_COLS + 2 * DIFF_QK_COLS + DIFF_V_COLS
SWA_OUT = SWA_Q_HEADS * HEAD_DIM
DIFF_OUT = DIFF_HEADS * DIFF_VDIM
MEM_LEN = 256
CROSS_HEADS = 4
CROSS_HEAD_DIM = D_MODEL // CROSS_HEADS
D_FF_2 = 4 * D_MODEL
ROPE_THETA_2 = 10000.0


def rms_norm_2(x, g, eps=NORM_EPS):
    xf = x.astype(jnp.float32)
    y = xf * lax.rsqrt(jnp.mean(xf * xf, axis=-1, keepdims=True) + eps)
    return (y * g.astype(jnp.float32)).astype(x.dtype)

def rope_tables(positions, dim):
    inv_freq = ROPE_THETA_2 ** (-jnp.arange(0, dim, 2, dtype=jnp.float32) / dim)
    ang = positions.astype(jnp.float32)[..., None] * inv_freq
    return jnp.cos(ang), jnp.sin(ang)

def apply_rope(x, cos, sin):
    shp = cos.shape[:2] + (1,) * (x.ndim - 3) + cos.shape[-1:]
    c = cos.reshape(shp).astype(x.dtype)
    s = sin.reshape(shp).astype(x.dtype)
    x1, x2 = jnp.split(x, 2, axis=-1)
    return jnp.concatenate([x1 * c - x2 * s, x2 * c + x1 * s], axis=-1)

def sliding_window_sink_attention(q, k, v, sinks):
    Bn, S = q.shape[0], q.shape[1]
    nb = S // BLOCK
    scale = HEAD_DIM ** -0.5
    qb = q.reshape(Bn, nb, BLOCK, SWA_KV_HEADS, SWA_GROUP, HEAD_DIM)
    kb = k.reshape(Bn, nb, BLOCK, SWA_KV_HEADS, HEAD_DIM)
    vb = v.reshape(Bn, nb, BLOCK, SWA_KV_HEADS, HEAD_DIM)
    pad = ((0, 0), (1, 0), (0, 0), (0, 0), (0, 0))
    kw = jnp.concatenate([jnp.pad(kb, pad)[:, :-1], kb], axis=2)
    vw = jnp.concatenate([jnp.pad(vb, pad)[:, :-1], vb], axis=2)
    s = jnp.einsum('bnqhgd,bnkhd->bnhgqk', qb, kw).astype(jnp.float32) * scale
    qi = jnp.arange(BLOCK)[:, None]
    kj = jnp.arange(2 * BLOCK)[None, :]
    rel = qi + BLOCK - kj
    band = (rel >= 0) & (rel < WINDOW_2)
    exists = (jnp.arange(nb)[:, None, None] * BLOCK + kj[None]) >= BLOCK
    valid = band[None] & exists
    s = jnp.where(valid[None, :, None, None], s, -jnp.inf)
    sink = sinks.astype(jnp.float32).reshape(SWA_KV_HEADS, SWA_GROUP)[None, None, :, :, None, None]
    m = jnp.maximum(jnp.max(s, axis=-1, keepdims=True), sink)
    e = jnp.exp(s - m)
    p = e / (jnp.sum(e, axis=-1, keepdims=True) + jnp.exp(sink - m))
    o = jnp.einsum('bnhgqk,bnkhd->bnqhgd', p.astype(v.dtype), vw)
    return o.reshape(Bn, S, SWA_OUT)

def differential_attention(q, k, v, lam):
    Bn, S = q.shape[0], q.shape[1]
    nb = S // Q_BLOCK
    scale = HEAD_DIM ** -0.5
    qb = q.reshape(Bn, nb, Q_BLOCK, DIFF_HEADS, 2, HEAD_DIM).swapaxes(0, 1)
    starts = jnp.arange(nb) * Q_BLOCK
    kpos = jnp.arange(S)

    def one_block(args):
        qblk, start = args
        s = jnp.einsum('bqhcd,bkhcd->bhcqk', qblk, k).astype(jnp.float32) * scale
        mask = kpos[None, :] <= (start + jnp.arange(Q_BLOCK))[:, None]
        s = jnp.where(mask, s, -jnp.inf)
        p = jax.nn.softmax(s, axis=-1)
        a = p[:, :, 0] - lam * p[:, :, 1]
        return jnp.einsum('bhqk,bkhe->bqhe', a.astype(v.dtype), v)

    o = lax.map(one_block, (qb, starts))
    return o.swapaxes(0, 1).reshape(Bn, S, DIFF_HEADS, DIFF_VDIM)

def cross_attention(h, m, w_q, w_kv, w_o):
    Bn, S = h.shape[0], h.shape[1]
    q = (h @ w_q).reshape(Bn, S, CROSS_HEADS, CROSS_HEAD_DIM)
    kv = (m @ w_kv).reshape(Bn, m.shape[1], 2, CROSS_HEADS, CROSS_HEAD_DIM)
    k, v = kv[:, :, 0], kv[:, :, 1]
    s = jnp.einsum('bshd,bmhd->bhsm', q, k).astype(jnp.float32) * CROSS_HEAD_DIM ** -0.5
    p = jax.nn.softmax(s, axis=-1)
    o = jnp.einsum('bhsm,bmhd->bshd', p.astype(v.dtype), v).reshape(Bn, S, D_MODEL)
    return o @ w_o

def second_inputs(seed: int = 0) -> dict:
    key = jax.random.key(seed)
    ks = jax.random.split(key, 24)
    f32 = jnp.float32
    L = DEPTH_2

    def w(k, shape, fan_in):
        return jax.random.normal(k, shape, f32) * fan_in ** -0.5

    def gain(k, shape):
        return 1.0 + 0.02 * jax.random.normal(k, shape, f32)

    x = jax.random.normal(ks[0], (BATCH, SEQ, D_MODEL), f32)
    mem = jax.random.normal(ks[1], (BATCH, MEM_LEN, D_MODEL), f32)
    positions = (jnp.arange(SEQ, dtype=jnp.int32)[None, :]
                 + jax.random.randint(ks[2], (BATCH, 1), 0, 1024, dtype=jnp.int32))
    return {
        "x": x,
        "mem": mem,
        "positions": positions,
        "g_mix": gain(ks[3], (L, D_MODEL)),
        "w_in": w(ks[4], (L, D_MODEL, IN_COLS), D_MODEL),
        "sinks": 0.5 * jax.random.normal(ks[5], (L, SWA_Q_HEADS), f32),
        "lambda_q1": 0.1 * jax.random.normal(ks[6], (L, HEAD_DIM), f32),
        "lambda_k1": 0.1 * jax.random.normal(ks[7], (L, HEAD_DIM), f32),
        "lambda_q2": 0.1 * jax.random.normal(ks[8], (L, HEAD_DIM), f32),
        "lambda_k2": 0.1 * jax.random.normal(ks[9], (L, HEAD_DIM), f32),
        "g_diff": gain(ks[10], (L, DIFF_VDIM)),
        "w_out": w(ks[11], (L, MIX_WIDTH, D_MODEL), MIX_WIDTH),
        "g_cross": gain(ks[12], (L, D_MODEL)),
        "g_mem": gain(ks[13], (L, D_MODEL)),
        "w_cq": w(ks[14], (L, D_MODEL, D_MODEL), D_MODEL),
        "w_ckv": w(ks[15], (L, D_MODEL, 2 * D_MODEL), D_MODEL),
        "w_co": w(ks[16], (L, D_MODEL, D_MODEL), D_MODEL),
        "g_mlp": gain(ks[17], (L, D_MODEL)),
        "w_up": w(ks[18], (L, D_MODEL, D_FF_2), D_MODEL),
        "w_down": w(ks[19], (L, D_FF_2, D_MODEL), D_FF_2),
        "g_final": gain(ks[20], (D_MODEL,)),
    }

def second_block(x, mem, positions, g_mix, w_in, sinks, lambda_q1, lambda_k1, lambda_q2, lambda_k2,
              g_diff, w_out, g_cross, g_mem, w_cq, w_ckv, w_co, g_mlp, w_up, w_down, g_final):
    Bn, S = x.shape[0], x.shape[1]
    cos, sin = rope_tables(positions, HEAD_DIM)
    splits = np.cumsum([SWA_Q_COLS, SWA_KV_COLS, SWA_KV_COLS, DIFF_QK_COLS, DIFF_QK_COLS])
    for l in range(DEPTH_2):
        h = rms_norm_2(x, g_mix[l])
        proj = h @ w_in[l]
        qa, ka, va, qd, kd, vd = jnp.split(proj, splits, axis=-1)
        qa = apply_rope(qa.reshape(Bn, S, SWA_KV_HEADS, SWA_GROUP, HEAD_DIM), cos, sin)
        ka = apply_rope(ka.reshape(Bn, S, SWA_KV_HEADS, HEAD_DIM), cos, sin)
        va = va.reshape(Bn, S, SWA_KV_HEADS, HEAD_DIM)
        out_a = sliding_window_sink_attention(qa, ka, va, sinks[l])

        lam_init = 0.8 - 0.6 * math.exp(-0.3 * l)
        lam = (jnp.exp(jnp.sum(lambda_q1[l].astype(jnp.float32) * lambda_k1[l].astype(jnp.float32)))
               - jnp.exp(jnp.sum(lambda_q2[l].astype(jnp.float32) * lambda_k2[l].astype(jnp.float32)))
               + lam_init)
        qd = apply_rope(qd.reshape(Bn, S, DIFF_HEADS, 2, HEAD_DIM), cos, sin)
        kd = apply_rope(kd.reshape(Bn, S, DIFF_HEADS, 2, HEAD_DIM), cos, sin)
        vd = vd.reshape(Bn, S, DIFF_HEADS, DIFF_VDIM)
        od = differential_attention(qd, kd, vd, lam)
        out_b = (rms_norm_2(od, g_diff[l]) * (1.0 - lam_init)).reshape(Bn, S, DIFF_OUT)

        x = x + jnp.concatenate([out_a, out_b], axis=-1) @ w_out[l]

        x = x + cross_attention(rms_norm_2(x, g_cross[l]), rms_norm_2(mem, g_mem[l]),
                                w_cq[l], w_ckv[l], w_co[l])

        u = rms_norm_2(x, g_mlp[l]) @ w_up[l]
        x = x + jnp.square(jax.nn.relu(u)) @ w_down[l]
    return rms_norm_2(x, g_final)


def setup_inputs(seed=0):
    out = dict(first_inputs(seed))
    for name, value in second_inputs(seed + 1).items():
        if name != "x":
            out[name + "_2"] = value
    return out


def reference(
    x, norm_gain, sb_w_qkv, sb_w_o, kv_norm, nsa_w_kv, cmp_pos, cmp_w1, cmp_w2, nsa_w_q,
    nsa_gate_b, nsa_w_o, mlp_w1, mlp_w2, final_norm, mem_2, positions_2, g_mix_2, w_in_2,
    sinks_2, lambda_q1_2, lambda_k1_2, lambda_q2_2, lambda_k2_2, g_diff_2, w_out_2, g_cross_2,
    g_mem_2, w_cq_2, w_ckv_2, w_co_2, g_mlp_2, w_up_2, w_down_2, g_final_2,
):
    x = first_block(
        x, norm_gain, sb_w_qkv, sb_w_o, kv_norm, nsa_w_kv, cmp_pos, cmp_w1, cmp_w2, nsa_w_q,
        nsa_gate_b, nsa_w_o, mlp_w1, mlp_w2, final_norm,
    )
    return second_block(
        x, mem_2, positions_2, g_mix_2, w_in_2, sinks_2, lambda_q1_2, lambda_k1_2, lambda_q2_2,
        lambda_k2_2, g_diff_2, w_out_2, g_cross_2, g_mem_2, w_cq_2, w_ckv_2, w_co_2, g_mlp_2,
        w_up_2, w_down_2, g_final_2,
    )


_drawn_inputs = setup_inputs


def setup_inputs(seed=0):
    import zlib

    import numpy as np

    out = dict(_drawn_inputs(seed))
    spreads = {}
    factors = {'kv_norm': 8.0,
     'nsa_gate_b': 4.53,
     'g_mix_2': 4.641,
     'sinks_2': 8.0,
     'lambda_q1_2': 6.379,
     'lambda_k1_2': 4.569,
     'lambda_k2_2': 4.039,
     'g_diff_2': 5.433,
     'g_cross_2': 8.0,
     'g_mem_2': 8.0,
     'g_mlp_2': 10.011,
     'g_final_2': 8.33}
    for name, (base, spread) in spreads.items():
        noise = np.random.default_rng([zlib.crc32(name.encode()), seed]).standard_normal(out[name].shape)
        drawn = base * np.exp(spread * noise) if base else spread * noise
        out[name] = __import__('jax').numpy.asarray(drawn.astype(out[name].dtype))
    for name, factor in factors.items():
        out[name] = (out[name] * factor).astype(out[name].dtype)
    return out
```

```python
import concourse.bass as bass
from concourse import mybir
from concourse.alu_op_type import AluOpType as ALU
from contextlib import ExitStack
import numpy as np

F32 = mybir.dt.float32
F32R = mybir.dt.float32r
I32 = mybir.dt.int32
ACT = mybir.ActivationFunctionType
AXL = mybir.AxisListType

P = 128
S = 512
D = 1024
KT = D // P
QT = S // P
MEM = 256
HD = 64
BLK = 256
CH = 4
NCMP = 31
NCP = 32
EPS = 1e-5
NEG = -1e30
BIG = 3e38
TWO_PI = 6.283185307179586
TP1 = 6.28125
TP2 = float(np.float32(np.round((TWO_PI - TP1) * 2.0 ** 20) / 2.0 ** 20))
TP3 = float(np.float32(TWO_PI - TP1 - TP2))
PI_SAFE = 3.1415925
EXP_MOST = 80.0
MAGIC = 12582912.0
LAM_INIT = 0.2

STAGES = [("sb_qkv", 12), ("sb_o", 4), ("mlp0", 32), ("kv", 6), ("cmp", 4), ("q", 4), ("gate", 1), ("nsa_o", 4),
          ("mlp1", 32), ("in", 9), ("out", 4), ("ckv", 8), ("cq", 4), ("co", 4), ("mlp2", 32)]
FIRST = {}
NBLK = 0
for _name, _n in STAGES:
    FIRST[_name] = NBLK
    NBLK += _n

GAINS = ["mix0", "mlp0", "kv", "mix1", "mlp1", "final1", "mix2", "mem", "cross", "mlp2", "final2"]

QOFF = {3: 0, 2: 512, 0: 896, 1: 1024}
KOFF = {0: 0, 1: 512, 3: 896, 2: 1024}
CW = 1280


def build_program(nc, dram, out, upto=None):
    b = FIRST
    last_block = NBLK if upto is None else upto
    with ExitStack() as ctx:
        base = [(nc.sbuf_base + 63) // 64 * 64]

        def place(name, shape, dt=F32, at=None):
            size = 4 * int(np.prod(shape[1:]))
            size = (size + 31) // 32 * 32
            if at is None:
                at = base[0]
                base[0] += size
            return nc.alloc_sbuf_tensor_at(name, shape, dt, offset=at)

        def sem(name):
            return ctx.enter_context(nc.semaphore(name))

        KB = 1024
        x = place("x_res", [P, KT, S])
        HOFF = base[0]
        h_hi = place("h_hi", [P, KT, S], F32R)
        h_lo = place("h_lo", [P, KT, S], F32R)
        w_raw = place("w_raw", [P, 2, KT, BLK])
        w_hi = place("w_hi", [P, 2, KT, BLK], F32R)
        w_lo = place("w_lo", [P, 2, KT, BLK], F32R)
        o_hi = place("o_hi", [P, KT, S], F32R)
        o_lo = place("o_lo", [P, KT, S], F32R)
        AOFF = base[0]
        base[0] += 48 * KB
        NOFF = base[0]
        nrm = place("nrm", [P, 2, S])
        rstd = place("rstd", [P, S])
        XOFF = base[0]
        v_slc = place("v_slc", [P, QT, 256])
        v_win = place("v_win", [P, QT, 256])
        k_cmp = place("k_cmp", [P, 4, NCP])
        v_cmp = place("v_cmp", [P, 4, HD])
        gates = place("gates", [P, QT, 48])
        pcmp = place("pcmp", [P, S])
        m_sb = place("m_sb", [P, S], at=XOFF)
        m_causal = place("m_causal", [P, S])
        m_swa = place("m_swa", [P, 2 * P])
        m_cmp = place("m_cmp", [P, QT, NCP])
        ident = place("ident", [P, P])
        ones = place("ones", [P, P])
        upper = place("upper", [P, P], at=XOFF + 4 * KB)
        rot1 = place("rot1", [P, P])
        rot2 = place("rot2", [P, P])
        cosT = place("cosT", [P, S])
        sinT = place("sinT", [P, S])
        gain = place("gain", [P, len(GAINS), KT])
        gate_b = place("gate_b", [P, 48])
        sinks = place("sinks", [P, 8])
        nsink = place("nsink", [P, 8])
        cpos = place("cpos", [P, 2, 16])
        w2c = place("w2c", [P, 2, 2, HD])
        anyv = place("anyv", [P, 4])
        invf = place("invf", [P, 1])
        gdiff = place("gdiff", [P, 1])
        neglam = place("neglam", [P, 1])
        small = place("small", [P, 2, 6, 4])
        stat_max, stat_nm, stat_sum, stat_rc, stat_fac, stat_sink = (small[:, :, k, :] for k in range(6))
        lamw = place("lamw", [P, 4, HD], at=NOFF)
        lams = place("lams", [P, 8], at=NOFF + 2 * KB)
        lamp = place("lamp", [P, HD], at=NOFF + 3 * KB)
        assert base[0] <= nc.sbuf_usable_end, (base[0], nc.sbuf_usable_end)

        sb_qk = place("sb_qk", [P, 16, S], at=AOFF)
        sb_v = place("sb_v", [P, QT, D], at=AOFF + 32 * KB)
        zs = place("zs", [P, 2, CW], at=HOFF)
        soft = place("soft", [P, CW], at=HOFF + 10 * KB)
        spl = place("spl", [P, CW], at=HOFF + 15 * KB)
        stick = place("stick", [P, 2, CW], at=HOFF + 20 * KB)
        sb_qs = place("sb_qs", [P, S], at=NOFF)
        sb_ks = place("sb_ks", [P, S], at=NOFF + 2 * KB)
        sb_vs = place("sb_vs", [P, QT, P], at=NOFF + 4 * KB)
        e_cmp = place("e_cmp", [P, 2, 4, S], at=AOFF)
        kv_nat = place("kv_nat", [P, 8, S], at=AOFF + 16 * KB)
        b_raw = place("b_raw", [P, 16, 4, NCMP], at=AOFF + 40 * KB)
        k_slc = place("k_slc", [P, 4, S], at=AOFF + 32 * KB)
        k_win = place("k_win", [P, 4, S], at=AOFF + 40 * KB)
        q_plain = place("q_plain", [P, KT, S], at=AOFF)
        q_rot = place("q_rot", [P, KT, S], at=AOFF + 16 * KB)
        probs = place("probs", [P, 2, CW], at=HOFF)
        probsT = place("probsT", [P, 2, CW], at=HOFF + 10 * KB)
        nq_rot = place("nq_rot", [P, 2, S], at=HOFF + 20 * KB)
        nq_plain = place("nq_plain", [P, 2, S], at=HOFF + 24 * KB)
        nk_slc = place("nk_slc", [P, S], at=HOFF + 28 * KB)
        nk_win = place("nk_win", [P, S], at=HOFF + 30 * KB)
        nv_slc = place("nv_slc", [P, QT, HD], at=NOFF)
        nv_win = place("nv_win", [P, QT, HD], at=NOFF + KB)
        nk_cmp = place("nk_cmp", [P, NCP], at=NOFF + 2 * KB)
        nv_cmp = place("nv_cmp", [P, HD], at=NOFF + 2 * KB + 256)
        cstat = place("cstat", [P, 4, 16], at=NOFF + 2 * KB + 512)
        cmpT = place("cmpT", [P, S], at=NOFF + 3 * KB)
        cpre = place("cpre", [P, 2, 2, 4 * NCMP], at=HOFF)
        cwork = place("cwork", [P, 2, 2, 4 * NCMP], at=HOFF + 2 * KB)
        cval = place("cval", [P, 2, 4, 4, NCP], at=HOFF + 6 * KB)
        rope_t = place("rope_t", [P, 2, S], at=NOFF)
        rope_i = place("rope_i", [P, S], I32, at=NOFF)
        inp = place("inp", [P, 13, S], at=AOFF)
        va = place("va", [P, QT, P], at=AOFF + 26 * KB)
        vd = place("vd", [P, QT, 512], at=AOFF + 28 * KB)
        ka_dup = place("ka_dup", [P, 2, S], at=AOFF + 36 * KB)
        od = place("od", [P, 4, S], at=AOFF + 40 * KB)
        aq_s = place("aq_s", [P, 2, S], at=HOFF + 20 * KB)
        ak_s = place("ak_s", [P, S], at=HOFF + 24 * KB)
        av_s = place("av_s", [P, QT, HD], at=NOFF)
        dq_s = place("dq_s", [P, S], at=HOFF + 26 * KB)
        dk_s = place("dk_s", [P, S], at=HOFF + 28 * KB)
        dv_s = place("dv_s", [P, QT, P], at=HOFF + 30 * KB)
        c_q = place("c_q", [P, KT, S], at=AOFF)
        c_k = place("c_k", [P, KT, MEM], at=AOFF + 16 * KB)
        c_v = place("c_v", [P, 2, D], at=AOFF + 24 * KB)
        mem = place("mem_in", [P, KT, MEM], at=AOFF + 32 * KB)
        cq_s = place("cq_s", [P, 4, S], at=HOFF + 20 * KB)
        ck_s = place("ck_s", [P, 4, MEM], at=HOFF + 28 * KB)
        cv_s = place("cv_s", [P, 2, 512], at=NOFF)

        ps = ctx.enter_context(nc.psum_tensor("ps", [P, 8, S], F32))
        flat = ps[:, :, :].rearrange("p a b -> p (a b)")
        sc = flat[:, 0:3 * S]
        pt = flat[:, 3 * S:6 * S]
        NB = 4

        raw_landed = [sem("raw_landed0"), sem("raw_landed1")]
        hi_ready, split_ready = sem("hi_ready"), sem("split_ready")
        tile_done, tile_free = sem("tile_done"), sem("tile_free")
        x_landed, const_landed, mem_landed, pos_landed = sem("x_landed"), sem("const_landed"), sem("mem_landed"), sem("pos_landed")
        out_stored, shifted, dup_k, dup_a = sem("out_stored"), sem("shifted"), sem("dup_k"), sem("dup_a")
        sq_ready, sq_used, std_ready, rstd_ready = sem("sq_ready"), sem("sq_used"), sem("std_ready"), sem("rstd_ready")
        y_ready, hhi_ready, h_ready, xn_ready = sem("y_ready"), sem("hhi_ready"), sem("h_ready"), sem("xn_ready")
        relu_ready, hid_y, hid_hi, hid_ready = sem("relu_ready"), sem("hid_y"), sem("hid_hi"), sem("hid_ready")
        (b_qk, b_v, z_done, zs_ready, nabs_ready, e_ready, l_ready, sp_ready, cum_done, arg_ready, a_ready, bpv_done,
         bhi_done, blo_done) = (sem("b_" + n) for n in ("qk", "v", "z", "zs", "nabs", "e", "l", "sp", "cum", "arg", "a",
                                                       "pv", "hi", "lo"))
        (st_qk, st_v, s_done, mx_ready, nm_ready, p_ready, esink_ready, den_ready, rc_ready, fac_ready, pn_ready, t_done,
         pt_copied, pv_done, ohi_done, olo_done) = (sem("s_" + n) for n in (
             "qk", "v", "s", "mx", "nm", "p", "esink", "den", "rc", "fac", "pn", "t", "ptc", "pv", "ohi", "olo"))
        b_added, b_hi, b_split, half_ready, cgel, cexp, ccmp, ccmp_done = (sem("c_" + n) for n in (
            "add", "bhi", "bsplit", "half", "gel", "exp", "cmp", "done"))
        rope_mm, rope_a, rope_b, rope_ready = sem("rope_mm"), sem("rope_a"), sem("rope_b"), sem("rope_ready")
        gsum, gexp, g_ready, lam_s, lam_e, consts_ready = sem("gsum"), sem("gexp"), sem("g_ready"), sem("lam_s"), sem("lam_e"), sem("consts_ready")
        trig_v, trig_a = sem("trig_v"), sem("trig_a")
        dsq, dsum, dstd, drstd, dy, dhi, dlo = (sem("d_" + n) for n in ("sq", "sum", "std", "rstd", "y", "hi", "lo"))

        def wait(eng, s, value):
            if not isinstance(value, int) or value > 0:
                eng.wait_ge(s, value)

        def f32(ap):
            return ap.bitcast(F32)

        print("left", nc.sbuf_usable_end - base[0])
        NORMS = {}
        splits = 0
        places = 0
        for i, (name, src, n, at, mode) in enumerate([
                ("mix0", x, S, 0, "split"), ("mlp0", x, S, b["mlp0"], "split"), ("kv", x, S, b["kv"], "split"),
                ("mix1", x, S, b["q"], "split"), ("mlp1", x, S, b["mlp1"], "split"), ("final1", x, S, b["in"], "place"),
                ("mix2", x, S, b["in"], "split"), ("mem", mem, MEM, b["ckv"], "split"), ("cross", x, S, b["cq"], "split"),
                ("mlp2", x, S, b["mlp2"], "split"), ("final2", x, S, NBLK, "place")]):
            NORMS[name] = dict(i=i, s=splits, pl=places, src=src, n=n, at=at, mode=mode, g=GAINS.index(name))
            splits += mode == "split"
            places += mode == "place"

        def tensor_norm(pe, name):
            k = NORMS[name]
            wait(pe, std_ready, k["i"])
            wait(pe, tile_free, 4 + 2 * k["at"])
            for t in range(KT):
                pe.wait_ge(sq_ready, KT * k["i"] + t + 1)
                pe.matmul(ps[:, NB, 0:k["n"]], ones[:, :], nrm[:, t % 2, 0:k["n"]], start=(t == 0),
                          stop=(t == KT - 1)).then_inc(sq_used, 1)

        def scalar_norm(act, name):
            k = NORMS[name]
            n = k["n"]
            if name == "mix0":
                act.wait_ge(x_landed, 16)
            elif name == "mem":
                act.wait_ge(mem_landed, 16)
            elif name == "mix2":
                act.wait_ge(xn_ready, KT)
            wait(act, tile_free, 4 + 2 * k["at"])
            wait(act, h_ready, KT * k["s"])
            for t in range(KT):
                if t >= 2:
                    act.wait_ge(sq_used, KT * k["i"] + t - 1)
                act.activation(nrm[:, t % 2, 0:n], k["src"][:, t, :], ACT.Square).then_inc(sq_ready, 1)
            act.wait_ge(sq_used, KT * k["i"] + KT)
            wait(act, rstd_ready, k["i"])
            act.activation(rstd[:, 0:n], ps[:, NB, 0:n], ACT.Sqrt, bias=eps_c[:, 0:1], scale=1.0 / D).then_inc(std_ready, 1)
            if k["mode"] == "split":
                wait(act, tile_done, 2 * k["at"])
                for t in range(KT):
                    act.wait_ge(y_ready, KT * k["s"] + t + 1)
                    act.activation(h_hi[:, t, 0:n], nrm[:, t % 2, 0:n], ACT.Copy).then_inc(hhi_ready, 1)

        def vector_norm(dve, name):
            k = NORMS[name]
            n = k["n"]
            g = gain[:, k["g"], :]
            dve.wait_ge(std_ready, k["i"] + 1)
            dve.reciprocal(rstd[:, 0:n], rstd[:, 0:n]).then_inc(rstd_ready, 1)
            dve.wait_ge(rstd_ready, k["i"] + 1)
            if k["mode"] == "place":
                for t in range(KT):
                    dve.scalar_tensor_tensor(out=x[:, t, :], in0=x[:, t, :], scalar=g[:, t:t + 1], in1=rstd[:, :],
                                             op0=ALU.mult, op1=ALU.mult).then_inc(xn_ready, 1)
                return

            def scaled(t):
                if t >= 2:
                    dve.wait_ge(h_ready, KT * k["s"] + t - 1)
                dve.scalar_tensor_tensor(out=nrm[:, t % 2, 0:n], in0=k["src"][:, t, :], scalar=g[:, t:t + 1],
                                         in1=rstd[:, 0:n], op0=ALU.mult, op1=ALU.mult).then_inc(y_ready, 1)
            scaled(0)
            for t in range(KT):
                if t + 1 < KT:
                    scaled(t + 1)
                dve.wait_ge(hhi_ready, KT * k["s"] + t + 1)
                dve.tensor_tensor(h_lo[:, t, 0:n], nrm[:, t % 2, 0:n], f32(h_hi[:, t, 0:n]), ALU.subtract).then_inc(h_ready, 1)

        def block_steps(eng, first, n, step):
            if n // 2 > 1:
                with eng.Fori(0, n // 2) as i:
                    step(i, 0)
                    step(i, 1)
            elif n // 2 == 1:
                step(0, 0)
                step(0, 1)
            if n % 2:
                step(n // 2, 0)

        def scalar_split(act, blk, par, half):
            act.wait_ge(raw_landed[par], 16 * half + 16)
            wait(act, tile_done, 2 * blk - 2)
            act.activation(w_hi[:, par, :, :], w_raw[:, par, :, :], ACT.Copy).then_inc(hi_ready, 1)

        def vector_split(dve, blk, par):
            dve.wait_ge(hi_ready, blk + 1)
            dve.tensor_tensor(w_lo[:, par, :, :], w_raw[:, par, :, :], f32(w_hi[:, par, :, :]), ALU.subtract).then_inc(split_ready, 1)

        def next_split(eng, which, first, i, u):
            nxt = first + u + 1
            if isinstance(i, int) and nxt + 2 * i >= last_block:
                return
            if which == "scalar":
                scalar_split(eng, nxt + 2 * i, nxt % 2, nxt // 2 + i)
            else:
                vector_split(eng, nxt + 2 * i, nxt % 2)

        def three(pe, o, l_hi, l_lo, r_hi, r_lo, first, last):
            pe.matmul(o, l_hi, r_hi, start=first, stop=False)
            pe.matmul(o, l_hi, r_lo, start=False, stop=False)
            return pe.matmul(o, l_lo, r_hi, start=False, stop=last)

        def tensor_block_T(pe, blk, par, r_hi, r_lo, n, ready=None, tiles=(0, 1)):
            pe.wait_ge(split_ready, blk + 1)
            for j in tiles:
                pe.wait_ge(tile_free, 2 * blk + j + 1)
                for k in range(KT):
                    if ready is not None and j == 0:
                        pe.wait_ge(ready[0], ready[1] + k + 1)
                    w = slice(j * P, j * P + P)
                    mm = three(pe, ps[:, 2 * par + j, 0:n], w_hi[:, par, k, w], w_lo[:, par, k, w],
                               r_hi[:, k, 0:n], r_lo[:, k, 0:n], k == 0, k == KT - 1)
                mm.then_inc(tile_done, 1)

        def tensor_block_N(pe, blk, par, plan):
            pe.wait_ge(split_ready, blk + 1)
            for j, parts in plan:
                pe.wait_ge(tile_free, 2 * blk + j + 1)
                for tt, c0, cn, at in parts:
                    for k in range(KT):
                        mm = three(pe, ps[:, 2 * par + j, at:at + cn], h_hi[:, k, tt * P:tt * P + P],
                                   h_lo[:, k, tt * P:tt * P + P], w_hi[:, par, k, c0:c0 + cn], w_lo[:, par, k, c0:c0 + cn],
                                   k == 0, k == KT - 1)
                mm.then_inc(tile_done, 1)

        WHOLE = [(j, [(2 * j + s, 0, BLK, s * BLK) for s in (0, 1)]) for j in (0, 1)]
        MEMORY = [(j, [(j, 0, BLK, 0)]) for j in (0, 1)]
        GATES = [(j, [(2 * j + s, 0, 48, s * 48) for s in (0, 1)]) for j in (0, 1)]
        VALUES_A = [(1, [(t, P, P, t * P) for t in range(QT)])]

        def tensor_linear_T(pe, first, n, r_hi, r_lo, tokens=S, ready=None):
            block_steps(pe, first, n, lambda i, u: tensor_block_T(
                pe, first + 2 * i + u, (first + u) % 2, r_hi, r_lo, tokens, ready))

        def tensor_linear_N(pe, first, n, plan):
            block_steps(pe, first, n, lambda i, u: tensor_block_N(pe, first + 2 * i + u, (first + u) % 2, plan))

        def scalar_linear(act, first, n):
            block_steps(act, first, n, lambda i, u: next_split(act, "scalar", first, i, u))

        def vector_linear(dve, first, n, evacuate):
            def step(i, u):
                next_split(dve, "vector", first, i, u)
                for j in (0, 1):
                    dve.wait_ge(tile_done, 2 * (first + 2 * i + u) + j + 1)
                    evacuate(i, u, j, 2 * ((first + u) % 2) + j).then_inc(tile_free, 1)
            block_steps(dve, first, n, step)

        def to_T(dve, dst, t0=0, n=S):
            return lambda i, u, j, bank: dve.tensor_copy(dst[:, t0 + 4 * i + 2 * u + j, 0:n], ps[:, bank, 0:n])

        def to_N(dve, dst, width=BLK):
            def evacuate(i, u, j, bank):
                at = width * (2 * i + u)
                d = dst[:, 2 * j:2 * j + 2, bass.ds(at, width)] if not isinstance(at, int) else dst[:, 2 * j:2 * j + 2, at:at + width]
                return dve.tensor_copy(d, ps[:, bank, 0:2 * width].rearrange("p (a b) -> p a b", a=2))
            return evacuate

        def add_to_x(dve):
            def evacuate(i, u, j, bank):
                t = 4 * i + 2 * u + j
                return dve.tensor_tensor(x[:, t, :], ps[:, bank, :], x[:, t, :], ALU.add)
            return evacuate

        def chunk_steps(eng, first, body):
            if first + 32 == NBLK:
                with eng.Fori(0, CH - 1) as c:
                    body(c)
                body(CH - 1)
            else:
                with eng.Fori(0, CH) as c:
                    body(c)

        def tensor_mlp(pe, m, norm):
            first = b["mlp%d" % m]

            def body(c):
                for q in range(4):
                    tensor_block_T(pe, first + 8 * c + q, (first + q) % 2, h_hi, h_lo, S, (h_ready, KT * NORMS[norm]["s"]))
                for q in range(4, 8):
                    tensor_block_T(pe, first + 8 * c + q, (first + q) % 2, o_hi, o_lo, S, (hid_ready, 8 * (CH * m + c)))
            chunk_steps(pe, first, body)

        def scalar_mlp(act, m):
            first = b["mlp%d" % m]

            def body(c):
                for q in range(8):
                    blk = first + 8 * c + q
                    if not (isinstance(c, int) and blk + 1 >= last_block):
                        scalar_split(act, blk + 1, (first + q + 1) % 2, (first + q + 1) // 2 + 4 * c)
                    if q >= 4:
                        continue
                    for j in (0, 1):
                        t = 2 * q + j
                        n = 8 * (CH * m + c) + t
                        act.wait_ge(tile_done, 2 * blk + j + 1)
                        if t >= 2:
                            act.wait_ge(hid_ready, n - 1)
                        act.activation(relu_buf[:, t % 2, :], ps[:, 2 * ((first + q) % 2) + j, :], ACT.Relu).then_inc(relu_ready, 1)
                        act.wait_ge(relu_ready, n + 1)
                        act.activation(o_hi[:, t, :], relu_buf[:, t % 2, :], ACT.Square).then_inc(hid_hi, 1)
            chunk_steps(act, first, body)

        def vector_mlp(dve, m):
            first = b["mlp%d" % m]

            def body(c):
                for q in range(8):
                    blk = first + 8 * c + q
                    if not (isinstance(c, int) and blk + 1 >= last_block):
                        vector_split(dve, blk + 1, (first + q + 1) % 2)
                    for j in (0, 1):
                        bank = ps[:, 2 * ((first + q) % 2) + j, :]
                        dve.wait_ge(tile_done, 2 * blk + j + 1)
                        if q >= 4:
                            t = 2 * (q - 4) + j
                            dve.tensor_tensor(x[:, t, :], bank, x[:, t, :], ALU.add).then_inc(tile_free, 1)
                            continue
                        t = 2 * q + j
                        n = 8 * (CH * m + c) + t
                        dve.wait_ge(relu_ready, n + 1)
                        wait(dve, hid_ready, n)
                        dve.scalar_tensor_tensor(out=hid_buf[:, 0, :], in0=bank, scalar=0.0, in1=relu_buf[:, t % 2, :],
                                                 op0=ALU.max, op1=ALU.mult).then_inc(tile_free, 1)
                        dve.wait_ge(tile_free, 2 * blk + j + 5)
                        dve.wait_ge(hid_hi, n + 1)
                        dve.tensor_tensor(o_lo[:, t, :], hid_buf[:, 0, :], f32(o_hi[:, t, :]), ALU.subtract).then_inc(hid_ready, 1)
            chunk_steps(dve, first, body)

        relu_buf = place("relu_buf", [P, 2, S], at=NOFF)
        hid_buf = place("hid_buf", [P, 1, S], at=NOFF + 4 * KB)
        eps_c = place("eps_c", [P, 1])
        assert base[0] <= nc.sbuf_usable_end, (base[0], nc.sbuf_usable_end)

        def pipelined(eng, iterations, units, parts):
            most = max(lag for lag, _ in parts)
            ahead = min(iterations, -(-most // units))

            def step(it, v):
                for lag, part in parts:
                    back, unit = divmod(v - lag, units)
                    if not isinstance(it, int) or 0 <= it + back < iterations:
                        part(it + back, unit)
            for it in range(ahead):
                for v in range(units):
                    step(it, v)
            if ahead < iterations:
                with eng.Fori(ahead, iterations) as it:
                    for v in range(units):
                        step(it, v)
            for v in range(most):
                step(iterations + v // units, v % units)

        SBH = 16

        def tensor_sb(pe):
            pe.wait_ge(tile_free, 4 + 2 * b["sb_o"])

            def z(it, u):
                n = 2 * it + u
                r = slice(HD * u, HD * u + HD)
                pe.wait_ge(b_qk, it + 1)
                wait(pe, zs_ready, n)
                for j in range(QT):
                    mm = pe.matmul(sc[:, KOFF[j]:KOFF[j] + S - P * j], sb_ks[r, P * j:P * j + P], sb_qs[r, P * j:S],
                                   start=True, stop=True)
                mm.then_inc(z_done, 1)

            def cum(it, u):
                n = 2 * it + u
                pe.wait_ge(sp_ready, n + 1)
                wait(pe, arg_ready, n)
                for j in range(QT):
                    for i in range(j, QT):
                        mm = pe.matmul(pt[:, KOFF[j] + P * (i - j):KOFF[j] + S - P * j], upper[:, :] if i == j else ones[:, :],
                                       spl[:, KOFF[i]:KOFF[i] + S - P * i], start=(i == j), stop=(i == QT - 1))
                mm.then_inc(cum_done, 1)

            def pv(it, u):
                n = 2 * it + u
                pe.wait_ge(a_ready, n + 1)
                pe.wait_ge(b_v, it + 1)
                wait(pe, blo_done, n)
                for j in range(QT):
                    mm = pe.matmul(ps[HD * u:HD * u + HD, 6 + u, P * j:S], sb_vs[:, j, HD * u:HD * u + HD],
                                   stick[:, u, KOFF[j]:KOFF[j] + S - P * j], start=(j == 0), stop=(j == QT - 1))
                mm.then_inc(bpv_done, 1)
            pipelined(pe, SBH // 2, 2, [(0, z), (3, pv), (1, cum)])

        def scalar_sb(act):
            def softplus(it, u):
                n = 2 * it + u
                act.wait_ge(nabs_ready, n + 1)
                act.activation(soft[:, :], soft[:, :], ACT.Exp).then_inc(e_ready, 1)
                act.wait_ge(e_ready, n + 1)
                act.activation(soft[:, :], soft[:, :], ACT.Ln, bias=1.0).then_inc(l_ready, 1)

            def weights(it, u):
                n = 2 * it + u
                act.wait_ge(arg_ready, n + 1)
                act.activation(stick[:, u, :], stick[:, u, :], ACT.Exp).then_inc(a_ready, 1)

            def high(it, u):
                n = 2 * it + u
                r = slice(HD * u, HD * u + HD)
                act.wait_ge(bpv_done, n + 1)
                act.activation(o_hi[r, it, :], ps[r, 6 + u, :], ACT.Copy).then_inc(bhi_done, 1)
            pipelined(act, SBH // 2, 2, [(3, high), (0, softplus), (1, weights)])

        def vector_sb(dve):
            def masked(it, u):
                n = 2 * it + u
                dve.wait_ge(z_done, n + 1)
                wait(dve, sp_ready, n)
                wait(dve, arg_ready, n - 1)
                for j in range(QT):
                    c = slice(KOFF[j], KOFF[j] + S - P * j)
                    ins = dve.scalar_tensor_tensor(out=zs[:, u, c], in0=sc[:, c], scalar=HD ** -0.5, in1=m_sb[:, 0:S - P * j],
                                                   op0=ALU.mult, op1=ALU.min)
                ins.then_inc(zs_ready, 1)
                dve.wait_ge(zs_ready, n + 1)
                dve.scalar_tensor_tensor(out=soft[:, :], in0=zs[:, u, :], scalar=-1.0, in1=zs[:, u, :], op0=ALU.mult,
                                         op1=ALU.min).then_inc(nabs_ready, 1)

            def argument(it, u):
                n = 2 * it + u
                dve.wait_ge(cum_done, n + 1)
                wait(dve, bpv_done, n - 1)
                dve.tensor_tensor(stick[:, u, :], zs[:, u, :], pt[:, 0:CW], ALU.subtract).then_inc(arg_ready, 1)

            def softplus(it, u):
                n = 2 * it + u
                dve.wait_ge(l_ready, n + 1)
                wait(dve, cum_done, n)
                dve.scalar_tensor_tensor(out=spl[:, :], in0=zs[:, u, :], scalar=0.0, in1=soft[:, :], op0=ALU.max,
                                         op1=ALU.add).then_inc(sp_ready, 1)

            def low(it, u):
                n = 2 * it + u
                r = slice(HD * u, HD * u + HD)
                dve.wait_ge(bhi_done, n + 1)
                dve.tensor_tensor(o_lo[r, it, :], ps[r, 6 + u, :], f32(o_hi[r, it, :]), ALU.subtract).then_inc(blo_done, 1)
            pipelined(dve, SBH // 2, 2, [(0, masked), (3, low), (0, softplus), (1, argument)])

        def pool_sb(pool):
            pool.wait_ge(tile_free, 4 + 2 * b["sb_o"])

            def queries_keys(p):
                wait(pool, z_done, 2 * p)
                pool.tensor_copy(sb_qs[:, :], sb_qk[:, p, :])
                pool.tensor_copy(sb_ks[:, :], sb_qk[:, 8 + p, :]).then_inc(b_qk, 1)

            def pair_values(p):
                wait(pool, bpv_done, 2 * p)
                src = sb_v[:, :, bass.ds(P * p, P)] if not isinstance(p, int) else sb_v[:, :, P * p:P * p + P]
                pool.tensor_copy(sb_vs[:, :, :], src).then_inc(b_v, 1)
            queries_keys(0)
            queries_keys(1)
            pair_values(0)
            with pool.Fori(2, SBH // 2) as p:
                queries_keys(p)
                pair_values(p - 1)
            pair_values(SBH // 2 - 1)

        CAUSAL_Q = [(t, QOFF[t], P * (t + 1)) for t in range(QT)]

        def heads_of(first_unit, iterations, units):
            return dict(base=first_unit, its=iterations, units=len(units), kinds=units)

        def scores_causal(q, k):
            return [(sc[:, QOFF[t]:QOFF[t] + P * (t + 1)], q[:, P * t:P * t + P], k[:, 0:P * (t + 1)], True, True) for t in range(QT)]

        def turns_causal(par):
            return [(pt[:, KOFF[j] + P * (t - j):KOFF[j] + P * (t - j) + P], probs[:, par, QOFF[t] + P * j:QOFF[t] + P * j + P])
                    for j in range(QT) for t in range(j, QT)]

        def values_causal(o, v, par, first, last):
            return [(o[:, P * j:S], v(j), probsT[:, par, KOFF[j]:KOFF[j] + S - P * j], first and j == 0, last and j == QT - 1)
                    for j in range(QT)]

        def nsa_units():
            def compressed(hh):
                r = slice(NCP * hh, NCP * hh + NCP)
                return (ps[HD * (hh % 2):HD * (hh % 2) + HD, 6 + hh % 2, :], nv_cmp[r, :], cmpT[r, :], True, False)
            units = [dict(par=0, head=0, branch=2, opens=True, closes=False, bank=6, rows=slice(0, HD),
                          scores=[(sc[:, S * (hh % 2) + 2 * NCP * t + NCP * (hh // 2):S * (hh % 2) + 2 * NCP * t + NCP * (hh // 2) + NCP],
                                   nq_plain[HD * (hh % 2):HD * (hh % 2) + HD, hh // 2, P * t:P * t + P],
                                   nk_cmp[HD * (hh % 2):HD * (hh % 2) + HD, :], True, True) for t in range(QT) for hh in range(4)],
                          turns=[(pt[:, P * t:P * t + P], pcmp[:, P * t:P * t + P]) for t in range(QT)],
                          values=[compressed(0)])]
            for hh in range(4):
                r = slice(HD * (hh % 2), HD * (hh % 2) + HD)
                o = ps[r, 6 + hh % 2, :]
                for br, (k, v) in enumerate([(nk_slc, nv_slc), (nk_win, nv_win)]):
                    par = len(units) % 2
                    first = [compressed(hh)] if br == 0 and hh > 0 else []
                    units.append(dict(
                        par=par, head=hh, branch=br, opens=(br == 0 and hh > 0), closes=(br == 1), bank=6 + hh % 2, rows=r,
                        scores=scores_causal(nq_rot[r, hh // 2, :], k[r, :]),
                        regions=[(t, QOFF[t], P * (t + 1), m_causal[:, S - P * (t + 1):S]) for t in range(QT)],
                        turns=turns_causal(par), copy=(P, CW),
                        values=first + values_causal(o, lambda j, v=v: v[:, j, :], par, False, br == 1)))
            return units

        SWQ = {0: 0, 1: 128, 2: 512, 3: 768}
        SWK = {0: 0, 1: 256, 2: 512, 3: 768}

        def swa_units():
            units = []
            for g in range(4):
                r = slice(HD * (g % 2), HD * (g % 2) + HD)
                par = g % 2
                o = ps[r, 6 + g % 2, :]
                scores, regions, turns, values = [], [], [], []
                for t in range(QT):
                    k0 = P * max(t - 1, 0)
                    w = P * (t + 1) - k0
                    scores.append((sc[:, SWQ[t]:SWQ[t] + w], aq_s[r, g // 2, P * t:P * t + P], ak_s[r, k0:k0 + w], True, True))
                    regions.append((t, SWQ[t], w, m_swa[:, 2 * P - w:2 * P]))
                    for j in range(max(t - 1, 0), t + 1):
                        at = SWK[j] + P * (t - j)
                        turns.append((pt[:, at:at + P], probs[:, par, SWQ[t] + P * j - k0:SWQ[t] + P * j - k0 + P]))
                        values.append((o[:, P * t:P * t + P], av_s[:, j, :], probsT[:, par, at:at + P], j == max(t - 1, 0), j == t))
                units.append(dict(par=par, head=g, branch=0, opens=True, closes=True, bank=6 + g % 2, rows=r, scores=scores,
                                  regions=regions, turns=turns, copy=(P, 7 * P), values=values))
            return units

        def diff_units():
            units = []
            for c in range(2):
                r = slice(HD * c, HD * c + HD)
                units.append(dict(par=c, head=0, branch=c, opens=(c == 0), closes=(c == 1), bank=6, rows=slice(0, P),
                                  scores=scores_causal(dq_s[r, :], dk_s[r, :]),
                                  regions=[(t, QOFF[t], P * (t + 1), m_causal[:, S - P * (t + 1):S]) for t in range(QT)],
                                  turns=turns_causal(c), copy=(P, CW),
                                  values=values_causal(ps[:, 6, :], lambda j: dv_s[:, j, :], c, c == 0, c == 1)))
            return units

        def cross_units():
            units = []
            for u in range(2):
                scores, values = [], []
                for t in range(QT):
                    for kc in range(2):
                        scores.append((sc[:, MEM * t:MEM * t + MEM], cq_s[:, 2 * u + kc, P * t:P * t + P], ck_s[:, 2 * u + kc, :],
                                       kc == 0, kc == 1))
                for mt in range(2):
                    for j in range(2):
                        values.append((ps[:, 6 + mt, :], cv_s[:, j, MEM * u + P * mt:MEM * u + P * mt + P],
                                       probsT[:, u, S * j:S * j + S], j == 0, j == 1))
                units.append(dict(par=u, head=u, branch=0, opens=True, closes=True, bank=None, rows=slice(0, P), scores=scores,
                                  regions=[(t, MEM * t, MEM, None) for t in range(QT)],
                                  turns=[(pt[:, S * j + P * t:S * j + P * t + P], probs[:, u, MEM * t + P * j:MEM * t + P * j + P])
                                         for j in range(2) for t in range(QT)],
                                  copy=(P, 2 * S), values=values))
            return units

        grid = lambda ap: ap.rearrange("p (a b c) -> p a b c", a=QT, b=4)
        rows_of = lambda ap: ap.rearrange("p (a b) -> p a b", b=NCP)
        cmp4 = lambda ap: ap.rearrange("p (a b) -> p a b", a=QT)

        def scalar_cmp_copy(act, a, it, n):
            act.wait_ge(t_done, n + 1)
            wait(act, pv_done, n - 1)
            act.activation(cmpT[:, :], pt[:, 0:S], ACT.Copy).then_inc(pt_copied, 1)

        def scalar_cmp_exp(act, it, n):
            act.wait_ge(nm_ready, n + 1)
            act.activation(pcmp[:, :], pcmp[:, :], ACT.Exp, scale=HD ** -0.5).then_inc(p_ready, 1)

        def vector_cmp_largest(dve, it, n):
            pc = pcmp[:, :]
            for odd in (0, 1):
                s = sc[:, S * odd:S * odd + 8 * NCP].rearrange("p (t h n) -> p t h n", t=QT, h=2)
                d = pc.rearrange("p (t h o n) -> p t h o n", t=QT, h=2, o=2)[:, :, :, odd, :]
                ins = dve.tensor_tensor(d, s, m_cmp[:, :, :].unsqueeze(2).broadcast_to([P, QT, 2, NCP]), ALU.add)
            ins.then_inc(mx_ready, 1)
            dve.wait_ge(mx_ready, n + 1)
            dve.tensor_reduce(cstat[:, 0, :], rows_of(pc), AXL.X, ALU.max).then_inc(cs_max, 1)
            dve.wait_ge(cs_max, it + 1)
            dve.tensor_tensor(rows_of(pc), rows_of(pc), cstat[:, 0, :].unsqueeze(2).broadcast_to([P, 16, NCP]),
                              ALU.subtract).then_inc(nm_ready, 1)

        def vector_cmp_normal(dve, it, n):
            pc = pcmp[:, :]
            dve.wait_ge(p_ready, n + 1)
            dve.tensor_reduce(cstat[:, 1, :], rows_of(pc), AXL.X, ALU.add).then_inc(cs_sum, 1)
            g = gates[:, :, span(4 * it, 4)]
            dve.tensor_tensor(cmp4(cstat[:, 2, :]), g, anyv[:, :].unsqueeze(2).broadcast_to([P, QT, 4]), ALU.mult).then_inc(cs_gate, 1)
            dve.wait_ge(cs_sum, it + 1)
            dve.reciprocal(cstat[:, 1, :], cstat[:, 1, :]).then_inc(rc_ready, 1)
            dve.wait_ge(rc_ready, n + 1)
            dve.wait_ge(cs_gate, it + 1)
            dve.tensor_tensor(cstat[:, 3, :], cstat[:, 1, :], cstat[:, 2, :], ALU.mult).then_inc(cs_fac, 1)
            dve.wait_ge(cs_fac, it + 1)
            dve.tensor_tensor(rows_of(pc), rows_of(pc), cstat[:, 3, :].unsqueeze(2).broadcast_to([P, 16, NCP]),
                              ALU.mult).then_inc(pn_ready, 1)

        ATT = {}
        n0 = o0 = i0 = 0
        for name, its, units, scale in [("nsa", 4, nsa_units(), HD ** -0.5), ("swa", 2, swa_units(), HD ** -0.5),
                                        ("diff", 4, diff_units(), HD ** -0.5), ("cross", 2, cross_units(), MEM ** -0.5)]:
            closes = sum(u["closes"] for u in units)
            ATT[name] = dict(n0=n0, o0=o0, i0=i0, its=its, units=units, scale=scale, closes=closes)
            n0 += its * len(units)
            o0 += its * closes
            i0 += its

        def unit_no(a, it, v):
            return a["n0"] + len(a["units"]) * it + v

        def output_no(a, it, v):
            return a["o0"] + a["closes"] * it + sum(u["closes"] for u in a["units"][:v])

        def tensor_attention(pe, name):
            a = ATT[name]
            U = a["units"]

            def scores(it, v):
                if v == 0:
                    pe.wait_ge(st_qk, a["i0"] + it + 1)
                wait(pe, mx_ready, unit_no(a, it, v))
                for o, l, r, first, last in U[v]["scores"]:
                    mm = pe.matmul(o, l, r, start=first, stop=last)
                mm.then_inc(s_done, 1)

            def turn(it, v):
                pe.wait_ge(pn_ready, unit_no(a, it, v) + 1)
                wait(pe, pt_copied, unit_no(a, it, v))
                for o, i in U[v]["turns"]:
                    mm = pe.transpose(o, i, ident[:, :])
                mm.then_inc(t_done, 1)

            def values(it, v):
                pe.wait_ge(pt_copied, unit_no(a, it, v) + 1)
                if v == 0:
                    pe.wait_ge(st_v, a["i0"] + it + 1)
                if U[v]["opens"]:
                    back = 1 if name in ("nsa", "swa") else 0
                    wait(pe, olo_done, output_no(a, it, v) - back)
                for o, l, r, first, last in U[v]["values"]:
                    mm = pe.matmul(o, l, r, start=first, stop=last)
                mm.then_inc(pv_done, 1)
            pipelined(pe, a["its"], len(U), [(0, scores), (2, turn), (3, values)])

        def scalar_attention(act, name):
            a = ATT[name]
            U = a["units"]

            def copy(it, v):
                n = unit_no(a, it, v)
                if name == "nsa" and v == 0:
                    scalar_cmp_copy(act, a, it, n)
                    return
                rows, width = U[v]["copy"]
                act.wait_ge(t_done, n + 1)
                wait(act, pv_done, n - 1)
                act.activation(probsT[0:rows, U[v]["par"], 0:width], pt[0:rows, 0:width], ACT.Copy).then_inc(pt_copied, 1)

            def expo(it, v):
                n = unit_no(a, it, v)
                par = U[v]["par"]
                if name == "nsa" and v == 0:
                    scalar_cmp_exp(act, it, n)
                    return
                act.wait_ge(nm_ready, n + 1)
                if name == "swa":
                    h = 4 * it + U[v]["head"]
                    sk = sinks[:, bass.ds(h, 1)] if not isinstance(h, int) else sinks[:, h:h + 1]
                    for t in range(QT):
                        ins = act.activation(stat_sink[:, par, t:t + 1], stat_nm[:, par, t:t + 1], ACT.Exp, bias=sk)
                for t, at, w, mask in U[v]["regions"]:
                    ins = act.activation(probs[:, par, at:at + w], probs[:, par, at:at + w], ACT.Exp,
                                         bias=stat_nm[:, par, t:t + 1], accum_out=stat_sum[:, par, t:t + 1])
                ins.then_inc(p_ready, 1)

            def high(it, v):
                if not U[v]["closes"]:
                    return
                act.wait_ge(pv_done, unit_no(a, it, v) + 1)
                r = U[v]["rows"]
                if name == "nsa":
                    ins = act.activation(o_hi[r, 2 * it + U[v]["head"] // 2, :], ps[r, U[v]["bank"], :], ACT.Copy)
                elif name == "swa":
                    ins = act.activation(o_hi[r, 2 * it + U[v]["head"] // 2, :], ps[r, U[v]["bank"], :], ACT.Copy)
                elif name == "diff":
                    ins = act.activation(od[:, it, 0:S // 2], ps[:, 6, 0:S // 2], ACT.Copy)
                else:
                    for mt in range(2):
                        ins = act.activation(o_hi[:, 4 * it + 2 * v + mt, :], ps[:, 6 + mt, :], ACT.Copy)
                ins.then_inc(ohi_done, 1)
            pipelined(act, a["its"], len(U), [(2, copy), (0, expo), (3, high)])

        def vector_attention(dve, name):
            a = ATT[name]
            U = a["units"]

            def largest(it, v):
                n = unit_no(a, it, v)
                par = U[v]["par"]
                dve.wait_ge(s_done, n + 1)
                wait(dve, t_done, n - 1)
                if name == "nsa" and v == 0:
                    vector_cmp_largest(dve, it, n)
                    return
                dve.sem_inc(begun)
                for t, at, w, mask in U[v]["regions"]:
                    if mask is None:
                        dve.tensor_scalar(probs[:, par, at:at + w], sc[:, at:at + w], a["scale"], None, ALU.mult)
                        ins = dve.tensor_reduce(stat_max[:, par, t:t + 1], sc[:, at:at + w], AXL.X, ALU.max)
                    else:
                        ins = dve.tensor_tensor_reduce(probs[:, par, at:at + w], sc[:, at:at + w], mask, a["scale"], -BIG,
                                                       ALU.add, ALU.max, stat_max[:, par, t:t + 1])
                ins.then_inc(mx_ready, 1)
                dve.wait_ge(mx_ready, n + 1)
                if name == "swa":
                    h = 4 * it + U[v]["head"]
                    sk = nsink[:, bass.ds(h, 1)] if not isinstance(h, int) else nsink[:, h:h + 1]
                    dve.tensor_scalar(stat_nm[:, par, :], stat_max[:, par, :], -1.0, sk, ALU.mult, ALU.min).then_inc(nm_ready, 1)
                else:
                    dve.tensor_scalar(stat_nm[:, par, :], stat_max[:, par, :], -a["scale"] if name == "cross" else -1.0, None,
                                      ALU.mult).then_inc(nm_ready, 1)

            def normal(it, v):
                n = unit_no(a, it, v)
                par = U[v]["par"]
                if name == "nsa" and v == 0:
                    vector_cmp_normal(dve, it, n)
                    return
                dve.wait_ge(p_ready, n + 1)
                total = stat_sum
                if name == "swa":
                    dve.tensor_tensor(stat_sum[:, par, :], stat_sum[:, par, :], stat_sink[:, par, :], ALU.add).then_inc(den_ready, 1)
                    dve.wait_ge(den_ready, n - a["n0"] + 1)
                dve.reciprocal(stat_rc[:, par, :], total[:, par, :]).then_inc(rc_ready, 1)
                dve.wait_ge(rc_ready, n + 1)
                fac = stat_fac
                if name == "nsa":
                    c = 16 * (U[v]["branch"] + 1)
                    c = c + 4 * it + U[v]["head"]
                    g = gates[:, :, bass.ds(c, 1)] if not isinstance(c, int) else gates[:, :, c:c + 1]
                    dve.tensor_tensor(stat_fac[:, par, :], stat_rc[:, par, :], g.rearrange("p a b -> p (a b)"), ALU.mult).then_inc(fac_ready, 1)
                    fn = 8 * it + v
                elif name == "diff":
                    dve.tensor_scalar(stat_fac[:, par, :], stat_rc[:, par, :], neglam[:, 0:1] if v == 1 else 1.0, None,
                                      ALU.mult).then_inc(fac_ready, 1)
                    fn = n - a["n0"] + 33
                else:
                    fac = stat_rc
                    fn = None
                if fn is not None:
                    dve.wait_ge(fac_ready, fn)
                for t, at, w, mask in U[v]["regions"]:
                    ins = dve.tensor_scalar(probs[:, par, at:at + w], probs[:, par, at:at + w], fac[:, par, t:t + 1], None, ALU.mult)
                ins.then_inc(pn_ready, 1)

            def low(it, v):
                if not U[v]["closes"]:
                    return
                r = U[v]["rows"]
                dve.wait_ge(ohi_done, output_no(a, it, v) + 1)
                if name in ("nsa", "swa"):
                    t = 2 * it + U[v]["head"] // 2
                    ins = dve.tensor_tensor(o_lo[r, t, :], ps[r, U[v]["bank"], :], f32(o_hi[r, t, :]), ALU.subtract)
                elif name == "diff":
                    ins = dve.tensor_copy(od[:, it, S // 2:S], ps[:, 6, S // 2:S])
                else:
                    for mt in range(2):
                        t = 4 * it + 2 * v + mt
                        ins = dve.tensor_tensor(o_lo[:, t, :], ps[:, 6 + mt, :], f32(o_hi[:, t, :]), ALU.subtract)
                ins.then_inc(olo_done, 1)
            pipelined(dve, a["its"], len(U), [(0, largest), (1, normal), (3, low)])

        cs_max, cs_sum, cs_gate, cs_fac = (sem("cs_" + n) for n in ("max", "sum", "gate", "fac"))
        begun = sem("begun")

        def pool_attention(pool, name, first, qk, vals):
            a = ATT[name]
            for s, value in first:
                pool.wait_ge(s, value)

            def queries_keys(it):
                wait(pool, s_done, a["n0"] + len(a["units"]) * it)
                for d, s in qk(it):
                    ins = pool.tensor_copy(d, s)
                ins.then_inc(st_qk, 1)

            def turn_values(it):
                wait(pool, pv_done, a["n0"] + len(a["units"]) * it)
                for d, s in vals(it):
                    ins = pool.tensor_copy(d, s)
                ins.then_inc(st_v, 1)
            late = 1 if len(a["units"]) < 3 else 0
            for it in range(1 + late):
                queries_keys(it)
            turn_values(0)
            if 1 + late < a["its"]:
                with pool.Fori(1 + late, a["its"]) as it:
                    queries_keys(it)
                    turn_values(it - late)
            for it in range(a["its"] - late, a["its"]):
                turn_values(it)

        def span(start, n):
            return bass.ds(start, n) if not isinstance(start, int) else slice(start, start + n)

        def pool_nsa(pool):
            pool_attention(pool, "nsa", [(tile_free, 4 + 2 * b["nsa_o"]), (rope_ready, 12), (g_ready, 1), (dup_k, 256), (ccmp_done, 2)],
                           lambda g: [(nq_rot[:, :, :], q_rot[:, span(2 * g, 2), :]), (nq_plain[:, :, :], q_plain[:, span(2 * g, 2), :]),
                                      (nk_slc[:, :], k_slc[:, g, :]), (nk_win[:, :], k_win[:, g, :]), (nk_cmp[:, :], k_cmp[:, g, :])],
                           lambda g: [(nv_slc[:, :, :], v_slc[:, :, span(HD * g, HD)]), (nv_win[:, :, :], v_win[:, :, span(HD * g, HD)]),
                                      (nv_cmp[:, :], v_cmp[:, g, :])])

        def pool_swa(pool):
            pool_attention(pool, "swa", [(tile_free, 4 + 2 * b["out"]), (rope_ready, 25), (dup_a, 64)],
                           lambda k: [(aq_s[:, :, :], inp[:, span(2 * k, 2), :]), (ak_s[:, :], ka_dup[:, k, :])],
                           lambda k: [(av_s[:, :, :], va[:, :, span(HD * k, HD)])])

        def pool_diff(pool):
            pool_attention(pool, "diff", [],
                           lambda h: [(dq_s[:, :], inp[:, 4 + h, :]), (dk_s[:, :], inp[:, 8 + h, :])],
                           lambda h: [(dv_s[:, :, :], vd[:, :, span(P * h, P)])])

        def pool_cross(pool):
            pool_attention(pool, "cross", [(tile_free, 4 + 2 * b["co"])],
                           lambda i: [(cq_s[:, :, :], c_q[:, span(4 * i, 4), :]), (ck_s[:, :, :], c_k[:, span(4 * i, 4), :])],
                           lambda i: [(cv_s[:, :, :], c_v[:, :, span(512 * i, 512)])])

        ROPES = {"k": (0, 4), "q": (4, 8), "in": (12, 13)}

        def tensor_rope(pe, name, src, rot, first):
            r0, n = ROPES[name]
            for s, value in first:
                pe.wait_ge(s, value)

            def tile(i, u):
                wait(pe, rope_b, r0 + 2 * i + u)
                pe.matmul(ps[:, 4 + (r0 + u) % 2, :], rot[:, :], src(2 * i + u), start=True, stop=True).then_inc(rope_mm, 1)
            block_steps(pe, 0, n, tile)

        def vector_rope(dve, name, src, dst):
            r0, n = ROPES[name]

            def tile(i, u):
                k = r0 + 2 * i + u
                wait(dve, rope_ready, k)
                dve.tensor_tensor(rope_t[:, 0, :], src(2 * i + u), cosT[:, :], ALU.mult).then_inc(rope_a, 1)
                dve.wait_ge(rope_mm, k + 1)
                dve.tensor_tensor(rope_t[:, 1, :], ps[:, 4 + (r0 + u) % 2, :], sinT[:, :], ALU.mult).then_inc(rope_b, 1)
                dve.wait_ge(rope_a, k + 1)
                dve.wait_ge(rope_b, k + 1)
                dve.tensor_tensor(dst(2 * i + u), rope_t[:, 0, :], rope_t[:, 1, :], ALU.add).then_inc(rope_ready, 1)
            block_steps(dve, 0, n, tile)

        k_nat = lambda t: kv_nat[:, 4 + t, :]
        q_src, q_dst = (lambda t: q_plain[:, t, :]), (lambda t: q_rot[:, t, :])
        in_tile = lambda t: inp[:, t, :]

        TC = 4 * NCMP

        def tensor_compress(pe):
            for c in range(2):
                for half in range(2):
                    blk = b["cmp"] + 2 * c + half
                    pe.wait_ge(b_split, c + 1)
                    pe.wait_ge(split_ready, blk + 1)
                    for j in (0, 1):
                        pe.wait_ge(tile_free, 2 * blk + j + 1)
                        for k in range(KT):
                            w = slice(j * P, j * P + P)
                            r = slice((16 * c + 8 * half + k) * TC, (16 * c + 8 * half + k + 1) * TC)
                            mm = three(pe, ps[:, 2 * (blk % 2) + j, 0:TC], w_hi[:, blk % 2, k, w], w_lo[:, blk % 2, k, w],
                                       bh[:, r], bl[:, r], k == 0, k == KT - 1)
                        mm.then_inc(tile_done, 1)
            pe.wait_ge(cgel, 7)
            for rows in (slice(0, HD), slice(HD, P)):
                for m in range(2):
                    pe.matmul(ps[rows, 5, 0:TC], w2c[:, 0, m, :], cwork[:, 0, m, :], start=(m == 0), stop=(m == 1))
            for g in range(4):
                for m in range(2):
                    mm = pe.matmul(ps[:, 6, HD * g:HD * g + HD], cval[:, m, g, :, :].rearrange("p a b -> p (a b)"),
                                   w2c[:, 1, m, :], start=(m == 0), stop=(m == 1))
            mm.then_inc(ccmp, 1)

        bh = o_hi[:, :, :].rearrange("p a b -> p (a b)")
        bl = o_lo[:, :, :].rearrange("p a b -> p (a b)")

        def pool_compress(pool):
            pool.wait_ge(tile_free, 4 + 2 * (b["kv"] + 2))
            pool.memset(k_cmp[:, :, :], 0.0).then_inc(half_ready, 1)
            pool.memset(e_cmp[:, :, :, S - 1:S], 0.0).then_inc(half_ready, 1)
            pool.wait_ge(half_ready, 2)
            for c in range(2):
                for g in range(4):
                    src = kv_nat[HD * (g % 2):HD * (g % 2) + HD, 2 * c + g // 2, :]
                    pool.dma_start(e_cmp[0:HD, c, g, :], src).then_inc(shifted, 16)
                    pool.dma_start(e_cmp[HD:P, c, g, 0:S - 1], src[:, 1:S]).then_inc(shifted, 16)
            pool.wait_ge(shifted, 256)
            for c in range(2):
                wait(pool, b_split, c)
                for g in range(4):
                    e = e_cmp[:, c, g, 0:16 * 32].rearrange("p (n j l) -> p j n l", j=8, l=2)
                    for half in range(2):
                        n = slice(half, half + NCMP)
                        pool.tensor_tensor(b_raw[:, 8 * half:8 * half + 8, g, :], e[:, :, n, 0],
                                           cpos[:, c, 8 * half:8 * half + 8].unsqueeze(2).broadcast_to([P, 8, NCMP]),
                                           ALU.add).then_inc(b_added, 1)
            pool.wait_ge(rope_ready, 4)
            pool.wait_ge(b_split, 2)
            for dst, t0 in ((k_slc, 4), (k_win, 6)):
                for g in range(4):
                    for half in range(2):
                        pool.dma_start(dst[HD * half:HD * half + HD, g, :],
                                       kv_nat[HD * (g % 2):HD * (g % 2) + HD, t0 + g // 2, :]).then_inc(dup_k, 16)

        def scalar_compress(act):
            raw = b_raw[:, :, :, :].rearrange("p a b c -> p (a b c)")
            for c in range(2):
                act.wait_ge(b_added, 8 * (c + 1))
                act.wait_ge(tile_done, 2 * b["kv"])
                act.activation(bh[:, 16 * TC * c:16 * TC * (c + 1)], raw, ACT.Copy).then_inc(b_hi, 1)
            scalar_linear(act, b["cmp"], 4)
            act.wait_ge(cgel, 4)
            act.activation(cexpb[:, :], cexpb[:, :], ACT.Exp).then_inc(cexp, 1)

        cexpb = place("cexpb", [P, 4 * TC], at=HOFF + 4 * KB)

        def vector_compress(dve):
            raw = b_raw[:, :, :, :].rearrange("p a b c -> p (a b c)")
            for c in range(2):
                dve.wait_ge(b_hi, c + 1)
                dve.tensor_tensor(bl[:, 16 * TC * c:16 * TC * (c + 1)], raw, f32(bh[:, 16 * TC * c:16 * TC * (c + 1)]),
                                  ALU.subtract).then_inc(b_split, 1)
            for c in range(2):
                for half in range(2):
                    blk = b["cmp"] + 2 * c + half
                    if blk + 1 < last_block:
                        vector_split(dve, blk + 1, (blk + 1) % 2)
                    for j in (0, 1):
                        dve.wait_ge(tile_done, 2 * blk + j + 1)
                        bank = ps[:, 2 * (blk % 2) + j, 0:TC]
                        if half == 0:
                            dve.tensor_copy(cpre[:, c, j, :], bank).then_inc(tile_free, 1)
                        else:
                            dve.wait_ge(tile_free, 4 + 2 * blk)
                            dve.tensor_tensor(cpre[:, c, j, :], bank, cpre[:, c, j, :], ALU.add).then_inc(tile_free, 1)
            u = cpre[:, :, :, :].rearrange("p a b c -> p (a b c)")
            w = cwork[:, :, :, :].rearrange("p a b c -> p (a b c)")
            dve.wait_ge(tile_free, 4 + 2 * b["q"])
            dve.memset(cval[:, :, :, :, NCMP:NCP], 0.0)
            dve.tensor_tensor(w, u, u, ALU.mult).then_inc(cgel, 1)
            dve.wait_ge(cgel, 1)
            dve.tensor_scalar(w, w, 0.044715, 1.0, ALU.mult, ALU.add).then_inc(cgel, 1)
            dve.wait_ge(cgel, 2)
            dve.tensor_tensor(cexpb[:, :], w, u, ALU.mult).then_inc(cgel, 1)
            dve.wait_ge(cgel, 3)
            dve.tensor_scalar(cexpb[:, :], cexpb[:, :], -2.0 * 0.7978845608028654, EXP_MOST, ALU.mult, ALU.min).then_inc(cgel, 1)
            dve.wait_ge(cexp, 1)
            dve.tensor_scalar(cexpb[:, :], cexpb[:, :], 1.0, None, ALU.add).then_inc(cgel, 1)
            dve.wait_ge(cgel, 5)
            dve.reciprocal(cexpb[:, :], cexpb[:, :]).then_inc(cgel, 1)
            dve.wait_ge(cgel, 6)
            half = 2 * TC
            dve.tensor_tensor(w[:, 0:half], cexpb[:, 0:half], u[:, 0:half], ALU.mult)
            for m in range(2):
                four = lambda ap: ap[:, half + TC * m:half + TC * (m + 1)].rearrange(
                    "p (g n) -> p g n", g=4).unsqueeze(2).broadcast_to([P, 4, 4, NCMP])
                ins = dve.tensor_tensor(cval[:, m, :, :, 0:NCMP], four(cexpb[:, :]), four(u), ALU.mult)
            ins.then_inc(cgel, 1)
            dve.wait_ge(ccmp, 1)
            dve.tensor_copy(k_cmp[:, :, 0:NCMP], ps[:, 5, 0:TC].rearrange("p (g n) -> p g n", g=4)).then_inc(ccmp_done, 1)
            dve.tensor_copy(v_cmp[:, :, :], ps[:, 6, 0:4 * HD].rearrange("p (g n) -> p g n", g=4)).then_inc(ccmp_done, 1)

        def tensor_dnorm(pe):
            for h in range(4):
                pe.wait_ge(dsq, h + 1)
                pe.matmul(ps[:, 5, :], ones[:, :], nrm[:, 0, :], start=True, stop=True).then_inc(dsum, 1)

        def scalar_dnorm(act):
            for h in range(4):
                act.wait_ge(olo_done, ATT["diff"]["o0"] + h + 1)
                wait(act, dhi, h)
                act.activation(nrm[:, 0, :], od[:, h, :], ACT.Square).then_inc(dsq, 1)
                act.wait_ge(dsum, h + 1)
                wait(act, dy, h)
                act.activation(rstd[:, :], ps[:, 5, :], ACT.Sqrt, bias=eps_c[:, 0:1], scale=1.0 / P).then_inc(dstd, 1)
                act.wait_ge(dy, h + 1)
                act.activation(o_hi[:, 4 + h, :], nrm[:, 1, :], ACT.Copy).then_inc(dhi, 1)

        def vector_dnorm(dve):
            for h in range(4):
                dve.wait_ge(dstd, h + 1)
                dve.reciprocal(rstd[:, :], rstd[:, :]).then_inc(drstd, 1)
                dve.wait_ge(drstd, h + 1)
                dve.scalar_tensor_tensor(out=nrm[:, 1, :], in0=od[:, h, :], scalar=gdiff[:, 0:1], in1=rstd[:, :],
                                         op0=ALU.mult, op1=ALU.mult).then_inc(dy, 1)
                dve.wait_ge(dhi, h + 1)
                dve.tensor_tensor(o_lo[:, 4 + h, :], nrm[:, 1, :], f32(o_hi[:, 4 + h, :]), ALU.subtract).then_inc(dlo, 1)

        def vector_trig(dve):
            done = [0]

            def link(ins):
                done[0] += 1
                ins.then_inc(trig_v, 1)
                dve.wait_ge(trig_v, done[0])
            dve.wait_ge(pos_landed, 16)
            ang, n = rope_t[:, 0, :], rope_t[:, 1, :]
            link(dve.tensor_copy(n, rope_i[:, :]))
            link(dve.tensor_scalar(ang, n, invf[:, 0:1], None, ALU.mult))
            for shift, add, dst in ((0.0, 0.0, sinT), (0.25, TWO_PI / 4, cosT)):
                link(dve.tensor_scalar(n, ang, 1.0 / TWO_PI, shift, ALU.mult, ALU.add))
                link(dve.tensor_scalar(n, n, MAGIC, None, ALU.add))
                link(dve.tensor_scalar(n, n, -MAGIC, None, ALU.add))
                link(dve.scalar_tensor_tensor(out=dst[:, :], in0=n, scalar=-TP1, in1=ang, op0=ALU.mult, op1=ALU.add))
                link(dve.scalar_tensor_tensor(out=dst[:, :], in0=n, scalar=-TP2, in1=dst[:, :], op0=ALU.mult, op1=ALU.add))
                link(dve.scalar_tensor_tensor(out=dst[:, :], in0=n, scalar=-TP3, in1=dst[:, :], op0=ALU.mult, op1=ALU.add))
                link(dve.tensor_scalar(dst[:, :], dst[:, :], add, PI_SAFE, ALU.add, ALU.min))
                link(dve.tensor_scalar(dst[:, :], dst[:, :], -PI_SAFE, None, ALU.max))

        def scalar_trig(act):
            act.wait_ge(trig_v, 10)
            act.activation(sinT[:, :], sinT[:, :], ACT.Sin).then_inc(trig_a, 1)
            act.wait_ge(trig_v, 18)
            act.activation(cosT[:, :], cosT[:, :], ACT.Sin).then_inc(trig_a, 1)

        CONSTS = [("m_sb", m_sb), ("m_causal", m_causal), ("m_swa", m_swa), ("m_cmp", m_cmp), ("ident", ident), ("ones", ones),
                  ("upper", upper), ("rot1", rot1), ("rot2", rot2), ("cos1", cosT), ("sin1", sinT), ("gains", gain),
                  ("gate_b", gate_b), ("sinks", sinks), ("cpos", cpos), ("w2c", w2c), ("anyv", anyv), ("invf", invf),
                  ("gdiff", gdiff), ("lamw", lamw), ("eps", eps_c)]

        def full(t):
            return t[tuple(slice(None) for _ in t.shape)]

        def vector_consts(dve):
            dve.wait_ge(const_landed, 16 * len(CONSTS))
            for k in range(2):
                dve.tensor_tensor_reduce(lamp[:, :], lamw[:, 2 * k, :], lamw[:, 2 * k + 1, :], 1.0, 0.0, ALU.mult, ALU.add,
                                         lams[:, k:k + 1]).then_inc(lam_s, 1)
                dve.wait_ge(lam_s, k + 1)
            dve.wait_ge(lam_e, 1)
            dve.tensor_tensor(lams[:, 4:5], lams[:, 3:4], lams[:, 2:3], ALU.subtract).then_inc(lam_s, 1)
            dve.wait_ge(lam_s, 3)
            dve.tensor_scalar(neglam[:, :], lams[:, 4:5], -LAM_INIT, None, ALU.add).then_inc(lam_s, 1)
            dve.tensor_scalar(nsink[:, :], sinks[:, :], -1.0, None, ALU.mult).then_inc(lam_s, 1)
            dve.tensor_scalar(gdiff[:, :], gdiff[:, :], 1.0 - LAM_INIT, None, ALU.mult).then_inc(lam_s, 1)
            dve.wait_ge(lam_s, 6)
            dve.engine_nop().then_inc(consts_ready, 1)

        def scalar_consts(act):
            act.wait_ge(lam_s, 2)
            act.activation(lams[:, 2:4], lams[:, 0:2], ACT.Exp).then_inc(lam_e, 1)
            act.wait_ge(consts_ready, 1)

        def vector_gates(dve):
            gb = gate_b[:, :].unsqueeze(1).broadcast_to([P, 2, 48])
            blk = b["gate"]
            next_split(dve, "vector", blk, 0, 0)
            for j in (0, 1):
                dve.wait_ge(tile_done, 2 * blk + j + 1)
                dve.tensor_tensor(gates[:, 2 * j:2 * j + 2, :], ps[:, 2 * (blk % 2) + j, 0:96].rearrange("p (a b) -> p a b", a=2), gb,
                                  ALU.add).then_inc(tile_free, 1)
            dve.wait_ge(tile_free, 4 + 2 * (blk + 1))
            dve.tensor_scalar(gates[:, :, :], gates[:, :, :], -1.0, EXP_MOST, ALU.mult, ALU.min).then_inc(gsum, 1)
            dve.wait_ge(gexp, 1)
            dve.tensor_scalar(gates[:, :, :], gates[:, :, :], 1.0, None, ALU.add).then_inc(gsum, 1)
            dve.wait_ge(gsum, 2)
            dve.reciprocal(gates[:, :, :], gates[:, :, :]).then_inc(g_ready, 1)

        def scalar_gates(act):
            next_split(act, "scalar", b["gate"], 0, 0)
            act.wait_ge(gsum, 1)
            act.activation(gates[:, :, :], gates[:, :, :], ACT.Exp).then_inc(gexp, 1)

        def stop(name):
            return upto is not None and FIRST[name] >= upto

        block = ctx.enter_context(nc.Block())

        @block.sync
        def _(sp):
            sp.dma_start(w_raw[:, 0, :, :], dram["wstream"][0]).then_inc(raw_landed[0], 16)
            sp.dma_start(w_raw[:, 1, :, :], dram["wstream"][1]).then_inc(raw_landed[1], 16)
            count = NBLK if upto is None else (upto + 2) // 2 * 2
            with sp.Fori(1, count // 2) as i:
                for u in (0, 1):
                    sp.wait_ge(split_ready, 2 * i + u - 1)
                    sp.dma_start(w_raw[:, u, :, :], dram["wstream"][2 * i + u]).then_inc(raw_landed[u], 16)
            if upto is None:
                for t in range(KT):
                    sp.wait_ge(xn_ready, KT + t + 1)
                    sp.dma_start(out[:, t, :], x[:, t, :]).then_inc(out_stored, 16)
                sp.wait_ge(out_stored, 16 * KT)

        @block.gpsimd
        def _(pool):
            pool_sb(pool)
            if stop("kv"):
                return
            pool_compress(pool)
            if stop("nsa_o"):
                return
            pool_nsa(pool)
            if stop("in"):
                return
            pool.wait_ge(tile_free, 4 + 2 * b["mlp1"])
            pool.wait_ge(xn_ready, KT)
            pool.dma_start(rope_i[:, :], dram["positions"]).then_inc(pos_landed, 16)
            pool.wait_ge(rope_ready, 25)
            for k in range(2):
                for half in range(2):
                    pool.dma_start(ka_dup[HD * half:HD * half + HD, k, :], inp[HD * k:HD * k + HD, 12, :]).then_inc(dup_a, 16)
            pool_swa(pool)
            pool_diff(pool)
            pool.wait_ge(tile_free, 4 + 2 * b["out"])
            pool.wait_ge(pv_done, ATT["cross"]["n0"])
            pool.wait_ge(ohi_done, ATT["cross"]["o0"])
            pool.dma_start(mem[:, :, :], dram["memT"]).then_inc(mem_landed, 16)
            pool_cross(pool)

        @block.tensor
        def _(pe):
            pe.wait_ge(const_landed, 16 * len(CONSTS))
            tensor_norm(pe, "mix0")
            ready = lambda name: (h_ready, KT * NORMS[name]["s"])
            tensor_linear_T(pe, b["sb_qkv"], 8, h_hi, h_lo, ready=ready("mix0"))
            tensor_linear_N(pe, b["sb_qkv"] + 8, 4, WHOLE)
            tensor_sb(pe)
            pe.wait_ge(blo_done, SBH)
            tensor_linear_T(pe, b["sb_o"], 4, o_hi, o_lo)
            tensor_norm(pe, "mlp0")
            tensor_mlp(pe, 0, "mlp0")
            if stop("kv"):
                return
            tensor_norm(pe, "kv")
            tensor_linear_T(pe, b["kv"], 4, h_hi, h_lo, ready=ready("kv"))
            tensor_linear_N(pe, b["kv"] + 4, 2, WHOLE)
            tensor_rope(pe, "k", k_nat, rot1, [(tile_free, 4 + 2 * b["cmp"])])
            tensor_compress(pe)
            tensor_norm(pe, "mix1")
            tensor_linear_T(pe, b["q"], 4, h_hi, h_lo, ready=ready("mix1"))
            tensor_block_N(pe, b["gate"], b["gate"] % 2, GATES)
            tensor_rope(pe, "q", q_src, rot1, [(tile_free, 4 + 2 * b["gate"])])
            pe.wait_ge(rope_ready, 12)
            if stop("nsa_o"):
                return
            tensor_attention(pe, "nsa")
            pe.wait_ge(olo_done, ATT["swa"]["o0"])
            tensor_linear_T(pe, b["nsa_o"], 4, o_hi, o_lo)
            tensor_norm(pe, "mlp1")
            tensor_mlp(pe, 1, "mlp1")
            if stop("in"):
                return
            tensor_norm(pe, "final1")
            tensor_norm(pe, "mix2")
            tensor_linear_T(pe, b["in"], 6, h_hi, h_lo, ready=ready("mix2"))
            blk = b["in"] + 6
            tensor_block_T(pe, blk, blk % 2, h_hi, h_lo, S, tiles=(0,))
            tensor_block_N(pe, blk, blk % 2, VALUES_A)
            tensor_linear_N(pe, b["in"] + 7, 2, WHOLE)
            tensor_rope(pe, "in", in_tile, rot2, [(tile_free, 4 + 2 * b["out"])])
            pe.wait_ge(rope_ready, 25)
            tensor_attention(pe, "swa")
            tensor_attention(pe, "diff")
            tensor_dnorm(pe)
            pe.wait_ge(dlo, 4)
            tensor_linear_T(pe, b["out"], 4, o_hi, o_lo)
            tensor_norm(pe, "mem")
            tensor_linear_T(pe, b["ckv"], 4, h_hi, h_lo, tokens=MEM, ready=ready("mem"))
            tensor_linear_N(pe, b["ckv"] + 4, 4, MEMORY)
            tensor_norm(pe, "cross")
            tensor_linear_T(pe, b["cq"], 4, h_hi, h_lo, ready=ready("cross"))
            pe.wait_ge(tile_free, 4 + 2 * b["co"])
            tensor_attention(pe, "cross")
            pe.wait_ge(olo_done, ATT["cross"]["o0"] + 4)
            tensor_linear_T(pe, b["co"], 4, o_hi, o_lo)
            tensor_norm(pe, "mlp2")
            tensor_mlp(pe, 2, "mlp2")
            tensor_norm(pe, "final2")

        @block.scalar
        def _(act):
            act.dma_start(x[:, :, :], dram["xT"]).then_inc(x_landed, 16)
            for name, t in CONSTS:
                act.dma_start(full(t), dram[name]).then_inc(const_landed, 16)
            scalar_consts(act)
            scalar_split(act, 0, 0, 0)
            scalar_norm(act, "mix0")
            scalar_linear(act, b["sb_qkv"], 12)
            act.preload_act_table_set("natural_log_exp_and_others")
            scalar_sb(act)
            scalar_linear(act, b["sb_o"], 4)
            scalar_norm(act, "mlp0")
            scalar_mlp(act, 0)
            if stop("kv"):
                return
            scalar_norm(act, "kv")
            scalar_linear(act, b["kv"], 6)
            scalar_compress(act)
            scalar_norm(act, "mix1")
            scalar_linear(act, b["q"], 4)
            scalar_gates(act)
            if stop("nsa_o"):
                return
            scalar_attention(act, "nsa")
            scalar_linear(act, b["nsa_o"], 4)
            scalar_norm(act, "mlp1")
            scalar_mlp(act, 1)
            if stop("in"):
                return
            scalar_norm(act, "final1")
            scalar_trig(act)
            scalar_norm(act, "mix2")
            scalar_linear(act, b["in"], 9)
            scalar_attention(act, "swa")
            scalar_attention(act, "diff")
            scalar_dnorm(act)
            scalar_linear(act, b["out"], 4)
            scalar_norm(act, "mem")
            scalar_linear(act, b["ckv"], 8)
            scalar_norm(act, "cross")
            scalar_linear(act, b["cq"], 4)
            scalar_attention(act, "cross")
            scalar_linear(act, b["co"], 4)
            scalar_norm(act, "mlp2")
            scalar_mlp(act, 2)
            scalar_norm(act, "final2")

        @block.vector
        def _(dve):
            for _ in range(4):
                dve.engine_nop().then_inc(tile_free, 1)
            vector_consts(dve)
            vector_split(dve, 0, 0)
            vector_norm(dve, "mix0")
            vector_linear(dve, b["sb_qkv"], 8, to_T(dve, sb_qk))
            vector_linear(dve, b["sb_qkv"] + 8, 4, to_N(dve, sb_v))
            vector_sb(dve)
            vector_linear(dve, b["sb_o"], 4, add_to_x(dve))
            vector_norm(dve, "mlp0")
            vector_mlp(dve, 0)
            if stop("kv"):
                return
            vector_norm(dve, "kv")
            vector_linear(dve, b["kv"], 4, to_T(dve, kv_nat))
            vector_linear(dve, b["kv"] + 4, 1, to_N(dve, v_slc))
            vector_linear(dve, b["kv"] + 5, 1, to_N(dve, v_win))
            vector_rope(dve, "k", k_nat, k_nat)
            vector_compress(dve)
            vector_norm(dve, "mix1")
            dve.wait_ge(dup_k, 256)
            vector_linear(dve, b["q"], 4, to_T(dve, q_plain))
            vector_gates(dve)
            vector_rope(dve, "q", q_src, q_dst)
            if stop("nsa_o"):
                return
            vector_attention(dve, "nsa")
            vector_linear(dve, b["nsa_o"], 4, add_to_x(dve))
            vector_norm(dve, "mlp1")
            vector_mlp(dve, 1)
            if stop("in"):
                return
            vector_norm(dve, "final1")
            vector_trig(dve)
            dve.wait_ge(trig_a, 2)
            vector_norm(dve, "mix2")
            vector_linear(dve, b["in"], 6, to_T(dve, inp))

            def ka_va(i, u, j, bank):
                if j == 0:
                    return dve.tensor_copy(inp[:, 12, :], ps[:, bank, :])
                return dve.tensor_copy(va[:, :, :], ps[:, bank, :].rearrange("p (a b) -> p a b", a=QT))
            vector_linear(dve, b["in"] + 6, 1, ka_va)
            vector_linear(dve, b["in"] + 7, 2, to_N(dve, vd))
            vector_rope(dve, "in", in_tile, in_tile)
            vector_attention(dve, "swa")
            vector_attention(dve, "diff")
            vector_dnorm(dve)
            vector_linear(dve, b["out"], 4, add_to_x(dve))
            vector_norm(dve, "mem")
            vector_linear(dve, b["ckv"], 4, to_T(dve, c_k, n=MEM))

            def memory_v(i, u, j, bank):
                return dve.tensor_copy(c_v[:, j, span(BLK * (2 * i + u), BLK)], ps[:, bank, 0:BLK])
            vector_linear(dve, b["ckv"] + 4, 4, memory_v)
            vector_norm(dve, "cross")
            vector_linear(dve, b["cq"], 4, to_T(dve, c_q))
            vector_attention(dve, "cross")
            vector_linear(dve, b["co"], 4, add_to_x(dve))
            vector_norm(dve, "mlp2")
            vector_mlp(dve, 2)
            vector_norm(dve, "final2")


def weight_blocks(w):
    n = w.shape[1] // BLK
    return [np.ascontiguousarray(w[:, BLK * i:BLK * (i + 1)].reshape(KT, P, BLK).transpose(1, 0, 2)) for i in range(n)]


def mlp_blocks(w1, w2):
    out = []
    for c in range(CH):
        out += weight_blocks(w1[:, D * c:D * (c + 1)]) + weight_blocks(w2[D * c:D * (c + 1), :])
    return out


def features(a):
    return np.ascontiguousarray(a.T.reshape(-1, P, a.shape[0]).transpose(1, 0, 2))


def rotation(period, half):
    m = np.zeros((P, P), np.float32)
    for p in range(P):
        d = p % period
        if d < half:
            m[p + half, p] = -1.0
        elif d < 2 * half:
            m[p - half, p] = 1.0
    return m


def constants():
    f = np.float32
    q, k = np.arange(P)[:, None], np.arange(P)[None, :]
    c = {}
    c["m_sb"] = np.full((P, S), BIG, f)
    c["m_sb"][:, :P] = np.where(k > q, f(BIG), f(NEG))
    c["m_causal"] = np.zeros((P, S), f)
    c["m_causal"][:, S - P:] = np.where(k <= q, f(0), f(NEG))
    c["m_swa"] = np.zeros((P, 2 * P), f)
    c["m_swa"][:, :P] = np.where(k > q, f(0), f(NEG))
    c["m_swa"][:, P:] = np.where(k <= q, f(0), f(NEG))
    t = P * np.arange(QT)[None, :, None] + np.arange(P)[:, None, None]
    n = np.arange(NCP)[None, None, :]
    c["m_cmp"] = np.where((16 * n + 31 <= t) & (n < NCMP), f(0), f(NEG)).astype(f)
    c["anyv"] = (t[:, :, 0] >= 31).astype(f)
    c["ident"] = np.eye(P, dtype=f)
    c["ones"] = np.ones((P, P), f)
    c["upper"] = (q >= k).astype(f)
    c["rot1"] = rotation(HD, 8)
    c["rot2"] = rotation(HD, 32)
    inv = (f(500000.0) ** (-np.arange(8, dtype=f) * f(2.0) / f(16))).astype(f)
    ang = (np.arange(S, dtype=f)[None, :] * inv[:, None]).astype(f)
    c["cos1"], c["sin1"] = np.ones((P, S), f), np.zeros((P, S), f)
    for p in range(P):
        if p % HD < 16:
            c["cos1"][p], c["sin1"][p] = np.cos(ang[p % 8]), np.sin(ang[p % 8])
    inv2 = (f(10000.0) ** (-np.arange(0, HD, 2, dtype=f) / f(HD))).astype(f)
    c["invf"] = np.ascontiguousarray(inv2[np.arange(P) % 32][:, None])
    c["eps"] = np.full((P, 1), EPS, f)
    return c


def layout(i):
    blocks = weight_blocks(i["sb_w_qkv"][0]) + weight_blocks(i["sb_w_o"][0]) + mlp_blocks(i["mlp_w1"][0], i["mlp_w2"][0])
    kv = weight_blocks(i["nsa_w_kv"])
    blocks += [kv[0], kv[1], kv[2], kv[4], kv[3], kv[5]]
    for c in range(2):
        blocks += weight_blocks(i["cmp_w1"][c][:D]) + weight_blocks(i["cmp_w1"][c][D:])
    wq = i["nsa_w_q"][0]
    blocks += weight_blocks(wq[:, :D])
    blocks += weight_blocks(np.concatenate([wq[:, D:], np.zeros((D, BLK - 48), wq.dtype)], axis=1))
    blocks += weight_blocks(i["nsa_w_o"][0]) + mlp_blocks(i["mlp_w1"][1], i["mlp_w2"][1])
    win = weight_blocks(i["w_in_2"][0])
    blocks += [win[0], win[1], win[3], win[4], win[5], win[6], win[2], win[7], win[8]]
    blocks += weight_blocks(i["w_out_2"][0]) + weight_blocks(i["w_ckv_2"][0]) + weight_blocks(i["w_cq_2"][0])
    blocks += weight_blocks(i["w_co_2"][0]) + mlp_blocks(i["w_up_2"][0], i["w_down_2"][0])
    assert len(blocks) == NBLK
    gains = [i["norm_gain"][0, 0], i["norm_gain"][0, 1], i["kv_norm"], i["norm_gain"][1, 0], i["norm_gain"][1, 1], i["final_norm"],
             i["g_mix_2"][0], i["g_mem_2"][0], i["g_cross_2"][0], i["g_mlp_2"][0], i["g_final_2"]]
    rows = lambda a: np.ascontiguousarray(np.broadcast_to(a, (P,) + a.shape))
    lam = np.stack([i["lambda_q1_2"][0], i["lambda_k1_2"][0], i["lambda_q2_2"][0], i["lambda_k2_2"][0]])
    d = dict(
        wstream=np.stack(blocks), xT=features(i["x"][0]), memT=features(i["mem_2"][0]),
        gains=np.ascontiguousarray(np.stack(gains).reshape(len(GAINS), KT, P).transpose(2, 0, 1)),
        gate_b=rows(i["nsa_gate_b"][0]), sinks=rows(i["sinks_2"][0]), lamw=rows(lam),
        cpos=np.ascontiguousarray(i["cmp_pos"].reshape(2, 16, P).transpose(2, 0, 1)),
        w2c=np.ascontiguousarray(i["cmp_w2"].reshape(2, 2, P, HD).transpose(2, 0, 1, 3)),
        gdiff=np.ascontiguousarray(i["g_diff_2"][0][:, None]), positions=rows(i["positions_2"][0]))
    d.update(constants())
    return d


def kernel(**inputs):
    import concourse.bacc as bacc
    from concourse.bass_utils import run_bass_kernel_spmd

    arrays = layout({k: np.asarray(v) for k, v in inputs.items()})
    nc = bacc.Bacc("TRN2", target_bir_lowering=False, num_devices=1)
    dram = {n: nc.dram_tensor("in_" + n, a.shape, mybir.dt.from_np(a.dtype), kind="ExternalInput").ap() for n, a in arrays.items()}
    out = nc.dram_tensor("out_T", (P, KT, S), F32, kind="ExternalOutput").ap()
    build_program(nc, dram, out)
    r = run_bass_kernel_spmd(nc, [{"in_" + n: a for n, a in arrays.items()}], core_ids=[0])
    got = r.results[0]["out_T"]
    return np.ascontiguousarray(got.transpose(1, 0, 2).reshape(D, S).T)[None]
```

```python
import concourse.bass as bass
from concourse import mybir
from concourse.alu_op_type import AluOpType as ALU
from contextlib import ExitStack
import numpy as np

F32 = mybir.dt.float32
F32R = mybir.dt.float32r
I32 = mybir.dt.int32
ACT = mybir.ActivationFunctionType
AXL = mybir.AxisListType

P = 128
S = 512
D = 1024
KT = D // P
QT = S // P
MEM = 256
HD = 64
BLK = 256
CH = 4
NCMP = 31
NCP = 32
EPS = 1e-5
NEG = -1e30
BIG = 3e38
TWO_PI = 6.283185307179586
TP1 = 6.28125
TP2 = float(np.float32(np.round((TWO_PI - TP1) * 2.0 ** 20) / 2.0 ** 20))
TP3 = float(np.float32(TWO_PI - TP1 - TP2))
PI_SAFE = 3.1415925
EXP_MOST = 80.0
MAGIC = 12582912.0
LAM_INIT = 0.2

STAGES = [("sb_qkv", 12), ("sb_o", 4), ("mlp0", 32), ("kv", 6), ("cmp", 4), ("q", 4), ("gate", 1), ("nsa_o", 4),
          ("mlp1", 32), ("in", 9), ("out", 4), ("ckv", 8), ("cq", 4), ("co", 4), ("mlp2", 32)]
FIRST = {}
NBLK = 0
for _name, _n in STAGES:
    FIRST[_name] = NBLK
    NBLK += _n

GAINS = ["mix0", "mlp0", "kv", "mix1", "mlp1", "final1", "mix2", "mem", "cross", "mlp2", "final2"]

QOFF = {3: 0, 2: 512, 0: 896, 1: 1024}
KOFF = {0: 0, 1: 512, 3: 896, 2: 1024}
CW = 1280


def build_program(nc, dram, out):
    b = FIRST
    with ExitStack() as ctx:
        base = [(nc.sbuf_base + 63) // 64 * 64]

        def place(name, shape, dt=F32, at=None):
            size = 4 * int(np.prod(shape[1:]))
            size = (size + 31) // 32 * 32
            if at is None:
                at = base[0]
                base[0] += size
            return nc.alloc_sbuf_tensor_at(name, shape, dt, offset=at)

        def sem(name):
            return ctx.enter_context(nc.semaphore(name))

        KB = 1024
        x = place("x_res", [P, KT, S])
        HOFF = base[0]
        h_hi = place("h_hi", [P, KT, S], F32R)
        h_lo = place("h_lo", [P, KT, S], F32R)
        w_raw = place("w_raw", [P, 2, KT, BLK])
        w_hi = place("w_hi", [P, 2, KT, BLK], F32R)
        w_lo = place("w_lo", [P, 2, KT, BLK], F32R)
        OOFF = base[0]
        o_hi = place("o_hi", [P, KT, S], F32R)
        o_lo = place("o_lo", [P, KT, S], F32R)
        AOFF = base[0]
        base[0] += 48 * KB
        NOFF = base[0]
        nrm = place("nrm", [P, 2, S])
        rstd = place("rstd", [P, S])
        XOFF = base[0]
        v_slc = place("v_slc", [P, QT, 256])
        v_win = place("v_win", [P, QT, 256])
        k_cmp = place("k_cmp", [P, 4, NCP])
        v_cmp = place("v_cmp", [P, 4, HD])
        gates = place("gates", [P, QT, 48])
        pcmp = place("pcmp", [P, S])
        m_sb = place("m_sb", [P, S], at=XOFF)
        m_causal = place("m_causal", [P, S])
        m_swa = place("m_swa", [P, 2 * P])
        m_cmp = place("m_cmp", [P, QT, NCP])
        ident = place("ident", [P, P])
        ones = place("ones", [P, P])
        upper = place("upper", [P, P], at=XOFF + 4 * KB)
        rot1 = place("rot1", [P, P])
        rot2 = place("rot2", [P, P])
        cosT = place("cosT", [P, S])
        sinT = place("sinT", [P, S])
        gain = place("gain", [P, len(GAINS), KT])
        gate_b = place("gate_b", [P, 48])
        sinks = place("sinks", [P, 8])
        nsink = place("nsink", [P, 8])
        cpos = place("cpos", [P, 2, 16])
        w2c = place("w2c", [P, 2, 2, HD])
        anyv = place("anyv", [P, 4])
        invf = place("invf", [P, 1])
        gdiff = place("gdiff", [P, 1])
        neglam = place("neglam", [P, 1])
        small = place("small", [P, 2, 6, 4])
        stat_max, stat_nm, stat_sum, stat_rc, stat_fac, stat_sink = (small[:, :, k, :] for k in range(6))
        eps_c = place("eps_c", [P, 2])
        rcol = place("rcol", [P, QT])
        gain12 = place("gain12", [P, KT])
        hid_buf = place("hid_buf", [P, 2, S], at=NOFF)
        lamw = place("lamw", [P, 4, HD], at=AOFF + 32 * KB)
        lams = place("lams", [P, 8], at=AOFF + 34 * KB)
        lamp = place("lamp", [P, HD], at=AOFF + 35 * KB)
        assert base[0] <= nc.sbuf_usable_end, (base[0], nc.sbuf_usable_end)

        sb_qk = place("sb_qk", [P, 16, S], at=AOFF)
        sb_v = place("sb_v", [P, QT, D], at=AOFF + 32 * KB)
        zs = place("zs", [P, 2, CW], at=HOFF)
        soft = place("soft", [P, CW], at=HOFF + 10 * KB)
        spl = place("spl", [P, CW], at=HOFF + 15 * KB)
        stick = place("stick", [P, 2, CW], at=HOFF + 20 * KB)
        sb_qs = place("sb_qs", [P, S], at=NOFF)
        sb_ks = place("sb_ks", [P, S], at=NOFF + 2 * KB)
        sb_vs = place("sb_vs", [P, QT, P], at=NOFF + 4 * KB)
        e_cmp = place("e_cmp", [P, 2, 4, S], at=AOFF)
        kv_nat = place("kv_nat", [P, 8, S], at=AOFF + 16 * KB)
        b_raw = place("b_raw", [P, 16, 4, NCMP], at=AOFF + 40 * KB)
        k_slc = place("k_slc", [P, 4, S], at=AOFF + 32 * KB)
        k_win = place("k_win", [P, 4, S], at=AOFF + 40 * KB)
        q_plain = place("q_plain", [P, KT, S], at=AOFF)
        q_rot = place("q_rot", [P, KT, S], at=AOFF + 16 * KB)
        probs = place("probs", [P, 2, CW], at=HOFF)
        probsT = place("probsT", [P, 2, CW], at=HOFF + 10 * KB)
        nq_rot = place("nq_rot", [P, 2, S], at=HOFF + 20 * KB)
        nq_plain = place("nq_plain", [P, 2, S], at=HOFF + 24 * KB)
        nk_slc = place("nk_slc", [P, S], at=HOFF + 28 * KB)
        nk_win = place("nk_win", [P, S], at=HOFF + 30 * KB)
        nv_slc = place("nv_slc", [P, QT, HD], at=NOFF)
        nv_win = place("nv_win", [P, QT, HD], at=NOFF + KB)
        nk_cmp = place("nk_cmp", [P, NCP], at=NOFF + 2 * KB)
        nv_cmp = place("nv_cmp", [P, HD], at=NOFF + 2 * KB + 256)
        cstat = place("cstat", [P, 4, 16], at=NOFF + 2 * KB + 512)
        cmpT = place("cmpT", [P, S], at=NOFF + 3 * KB)
        cpre, cwork, cexpb = (place("c" + n, [P, 2 * BLK], at=OOFF + 2 * i * KB) for i, n in enumerate(("pre", "work", "expb")))
        cact = place("cact", [P, 2, 4 * NCMP], at=OOFF + 6 * KB)
        cval = place("cval", [P, 2, 4, 4, NCP], at=OOFF + 16 * KB)
        rope_t = place("rope_t", [P, 2, S], at=NOFF)
        rope_i = place("rope_i", [P, S], I32, at=NOFF)
        inp = place("inp", [P, 13, S], at=AOFF)
        va = place("va", [P, QT, P], at=AOFF + 26 * KB)
        vd = place("vd", [P, QT, 512], at=AOFF + 28 * KB)
        ka_dup = place("ka_dup", [P, 2, S], at=AOFF + 36 * KB)
        od = place("od", [P, 4, S], at=AOFF + 40 * KB)
        dq_s = place("dq_s", [P, S], at=HOFF + 26 * KB)
        dk_s = place("dk_s", [P, S], at=HOFF + 28 * KB)
        dv_s = place("dv_s", [P, QT, P], at=HOFF + 30 * KB)
        d_sq = place("d_sq", [P, S], at=XOFF)
        d_y = place("d_y", [P, S], at=XOFF + 2 * KB)
        c_q = place("c_q", [P, KT, S], at=AOFF)
        c_k = place("c_k", [P, KT, MEM], at=AOFF + 16 * KB)
        c_v = place("c_v", [P, 2, D], at=AOFF + 24 * KB)
        mem = place("mem_in", [P, KT, MEM], at=AOFF + 32 * KB)
        m_lo = place("m_lo", [P, KT, MEM], F32R, at=AOFF + 4 * KB)
        m_hi = place("m_hi", [P, KT, MEM], F32R, at=AOFF + 40 * KB)
        macc = place("macc", [P, MEM], at=AOFF)
        mrstd = place("mrstd", [P, MEM], at=AOFF + KB)

        ps = ctx.enter_context(nc.psum_tensor("ps", [P, 8, S], F32))
        flat = ps[:, :, :].rearrange("p a b -> p (a b)")
        sc = flat[:, 0:3 * S]
        pt = flat[:, 3 * S:6 * S]

        raw_landed = [sem("raw_landed0"), sem("raw_landed1")]
        hi_ready, split_ready = sem("hi_ready"), sem("split_ready")
        tile_done, tile_free = sem("tile_done"), sem("tile_free")
        x_landed = [sem("x_landed%d" % i) for i in range(4)]
        first_landed, const_landed, mem_landed, pos_landed = sem("first_landed"), sem("const_landed"), sem("mem_landed"), sem("pos_landed")
        out_stored, shifted, dup_k, dup_a = sem("out_stored"), sem("shifted"), sem("dup_k"), sem("dup_a")
        sq_ready, acc_ready, sum_done = sem("sq_ready"), sem("acc_ready"), sem("sum_done")
        std_ready, rstd_ready, rhi_ready, r_ready = sem("std_ready"), sem("rstd_ready"), sem("rhi_ready"), sem("r_ready")
        hhi_ready, h_ready, xn_ready = sem("hhi_ready"), sem("h_ready"), sem("xn_ready")
        hid_y, hid_hi, hid_ready = sem("hid_y"), sem("hid_hi"), sem("hid_ready")
        (b_qk, b_v, z_done, zs_ready, nabs_ready, e_ready, l_ready, sp_ready, cum_done, arg_ready, a_ready, bpv_done,
         bhi_done, blo_done) = (sem("b_" + n) for n in ("qk", "v", "z", "zs", "nabs", "e", "l", "sp", "cum", "arg", "a",
                                                       "pv", "hi", "lo"))
        (st_qk, st_v, s_done, mx_ready, nm_ready, p_ready, den_ready, rc_ready, fac_ready, pn_ready, t_done,
         pt_copied, pv_done, ohi_done, olo_done) = (sem("s_" + n) for n in (
             "qk", "v", "s", "mx", "nm", "p", "den", "rc", "fac", "pn", "t", "ptc", "pv", "ohi", "olo"))
        b_added, b_hi, b_split, half_ready, cgel, cexp, ccmp, ccmp_done = (sem("c_" + n) for n in (
            "add", "bhi", "bsplit", "half", "gel", "exp", "cmp", "done"))
        cturned = sem("c_turned")
        rope_mm, rope_a, rope_b, rope_ready = sem("rope_mm"), sem("rope_a"), sem("rope_b"), sem("rope_ready")
        gsum, gexp, g_ready, lam_s, lam_e, consts_ready = sem("gsum"), sem("gexp"), sem("g_ready"), sem("lam_s"), sem("lam_e"), sem("consts_ready")
        trig_v, trig_a = sem("trig_v"), sem("trig_a")
        dsq, dsum, dstd, drstd, dy, dhi, dlo = (sem("d_" + n) for n in ("sq", "sum", "std", "rstd", "y", "hi", "lo"))

        def wait(eng, s, value):
            if not isinstance(value, int) or value > 0:
                eng.wait_ge(s, value)

        def f32(ap):
            return ap.bitcast(F32)

        def span(start, n):
            return bass.ds(start, n) if not isinstance(start, int) else slice(start, start + n)

        def norm(first, splits, squares, parts):
            return dict(first=first, splits=splits, squares=squares, parts=parts)

        sq, acc, acc2 = nrm[:, 0, :], nrm[:, 1, :], rstd[:, :]
        g_of = lambda name: gain[:, GAINS.index(name), :]
        x_split = lambda g: (x, S, g, h_hi, h_lo)
        NORMS = dict(
            mix0=norm(None, [x_split(g_of("mix0"))], [(x, S, None, acc)], "TN"),
            mlp0=norm(b["sb_o"], [x_split(g_of("mlp0"))], [(x, S, None, acc)], "T"),
            kv=norm(b["kv"] - 4, [x_split(g_of("kv"))], [(x, S, None, acc)], "TN"),
            mlp1=norm(b["nsa_o"], [x_split(g_of("mlp1"))], [(x, S, None, acc)], "T"),
            mix2=norm(b["in"] - 4, [x_split(gain12)], [(x, S, None, acc), (x, S, g_of("final1"), acc2)], "double"),
            cross=norm(b["out"], [(mem, MEM, g_of("mem"), m_hi, m_lo), x_split(g_of("cross"))],
                       [(mem, MEM, None, macc[:, :]), (x, S, None, acc)], "memory"),
            mlp2=norm(b["co"], [x_split(g_of("mlp2"))], [(x, S, None, acc)], "T"),
            final2=norm(NBLK - 4, [], [(x, S, None, acc)], "T"))
        counts = [0, 0, 0]
        for i, k in enumerate(NORMS.values()):
            k.update(i=i, h0=counts[0], s0=counts[1], a0=counts[2])
            counts[0] += KT * len(k["splits"])
            counts[1] += KT * len(k["squares"])
            counts[2] += (KT - 1) * len(k["squares"]) + (k["parts"] == "double")
            k["a1"] = counts[2]

        def scalar_tile(act, name, t, squares=True, splits=True):
            k = NORMS[name]
            if name == "mix0":
                act.wait_ge(x_landed[t // 2], 16)
            else:
                act.wait_ge(tile_free, 4 + 2 * k["first"] + t + 1)
            if name == "cross":
                act.wait_ge(mem_landed, 16)
            for src, n, g, hi, lo in k["splits"] if splits else []:
                act.activation(hi[:, t, 0:n], src[:, t, :], ACT.Copy, scale=g[:, t:t + 1]).then_inc(hhi_ready, 1)
            m = len(k["squares"])
            for p, (src, n, g, into) in enumerate(k["squares"] if squares else []):
                if t > 0:
                    wait(act, acc_ready, k["a0"] + m * (t - 1) + p)
                act.activation((into if t == 0 else sq)[:, 0:n], src[:, t, :], ACT.Square,
                               scale=1.0 if g is None else g[:, t:t + 1]).then_inc(sq_ready, 1)

        def vector_tile(dve, name, t, squares=True, splits=True):
            k = NORMS[name]
            m = len(k["splits"])
            for p, (src, n, g, hi, lo) in enumerate(k["splits"] if splits else []):
                dve.wait_ge(hhi_ready, k["h0"] + m * t + p + 1)
                dve.scalar_tensor_tensor(out=lo[:, t, 0:n], in0=src[:, t, :], scalar=g[:, t:t + 1], in1=f32(hi[:, t, 0:n]),
                                         op0=ALU.mult, op1=ALU.subtract).then_inc(h_ready, 1)
            m = len(k["squares"])
            for p, (src, n, g, into) in enumerate(k["squares"] if squares else []):
                dve.wait_ge(sq_ready, k["s0"] + m * t + p + 1)
                if t > 0:
                    wait(dve, acc_ready, k["a0"] + m * (t - 1) + p)
                    dve.tensor_tensor(into[:, 0:n], into[:, 0:n], sq[:, 0:n], ALU.add).then_inc(acc_ready, 1)
            if k["parts"] == "double" and t == KT - 1:
                dve.wait_ge(acc_ready, k["a1"] - 1)
                dve.scalar_tensor_tensor(out=acc2, in0=acc, scalar=EPS, in1=acc2, op0=ALU.mult, op1=ALU.add).then_inc(acc_ready, 1)

        def tensor_root(pe, name):
            k = NORMS[name]
            wait(pe, std_ready, k["i"])
            pe.wait_ge(acc_ready, k["a1"])
            mm = pe.matmul(ps[:, 4, :], ones[:, :], acc, start=True, stop=True)
            columns, tokens = acc, QT
            if k["parts"] == "double":
                pe.matmul(ps[:, 5, :], ones[:, :], acc2, start=True, stop=True)
                columns = acc2
            if k["parts"] == "memory":
                pe.matmul(ps[:, 5, 0:MEM], ones[:, :], macc[:, :], start=True, stop=True)
                columns, tokens = macc, 2
            if k["parts"] != "T":
                for t in range(tokens):
                    mm = pe.matmul(ps[:, 6, t:t + 1], columns[:, P * t:P * t + P], ones[:, 0:1], start=True, stop=True)
            mm.then_inc(sum_done, 1)

        def scalar_root(act, name):
            k = NORMS[name]
            if name == "mix0":
                for t in range(KT):
                    scalar_tile(act, name, t, splits=False)
            act.wait_ge(sum_done, k["i"] + 1)
            root = lambda dst, src, e=0: act.activation(dst, src, ACT.Sqrt, bias=eps_c[:, e:e + 1], scale=1.0 / D)
            if k["parts"] == "double":
                root(sq, ps[:, 4, :])
                root(rcol[:, :], ps[:, 6, 0:QT], 1)
                root(rstd[:, :], ps[:, 5, :], 1).then_inc(std_ready, 1)
                return
            if k["parts"] == "memory":
                root(mrstd[:, :], ps[:, 5, 0:MEM])
                root(rcol[:, 0:2], ps[:, 6, 0:2])
            if k["parts"] == "TN":
                root(rcol[:, :], ps[:, 6, 0:QT])
            root(rstd[:, :], ps[:, 4, :]).then_inc(std_ready, 1)

        def vector_root(dve, name):
            k = NORMS[name]
            if name == "mix0":
                for t in range(KT):
                    vector_tile(dve, name, t, splits=False)
            dve.wait_ge(std_ready, k["i"] + 1)
            if k["parts"] == "double":
                dve.reciprocal(sq, sq)
            if k["parts"] == "memory":
                dve.reciprocal(mrstd[:, :], mrstd[:, :])
            if k["parts"] != "T":
                n = 2 if k["parts"] == "memory" else QT
                dve.reciprocal(rcol[:, 0:n], rcol[:, 0:n])
            dve.reciprocal(rstd[:, :], rstd[:, :]).then_inc(rstd_ready, 1)
            dve.wait_ge(rstd_ready, k["i"] + 1)

        def vector_place(dve, name, root):
            for t in range(KT):
                dve.scalar_tensor_tensor(out=x[:, t, :], in0=x[:, t, :], scalar=g_of(name)[:, t:t + 1], in1=root,
                                         op0=ALU.mult, op1=ALU.mult).then_inc(xn_ready, 1)

        def scalar_resplit(act):
            act.wait_ge(tile_done, 2 * b["cmp"])
            for t in range(KT):
                act.activation(h_hi[:, t, :], x[:, t, :], ACT.Copy, scale=g_of("mix1")[:, t:t + 1]).then_inc(rhi_ready, 1)

        def vector_resplit(dve):
            for t in range(KT):
                dve.wait_ge(rhi_ready, t + 1)
                dve.scalar_tensor_tensor(out=h_lo[:, t, :], in0=x[:, t, :], scalar=g_of("mix1")[:, t:t + 1],
                                         in1=f32(h_hi[:, t, :]), op0=ALU.mult, op1=ALU.subtract).then_inc(r_ready, 1)

        def block_steps(eng, n, step, ahead=0):
            if n // 2 - ahead < 2:
                ahead = n // 2
            for i in range(ahead):
                step(i, 0)
                step(i, 1)
            if ahead < n // 2:
                with eng.Fori(ahead, n // 2) as i:
                    step(i, 0)
                    step(i, 1)
            if n % 2:
                step(n // 2, 0)

        def scalar_split(act, blk, par, half):
            act.wait_ge(raw_landed[par], 16 * half + 16)
            wait(act, tile_done, 2 * blk - 2)
            act.activation(w_hi[:, par, :, :], w_raw[:, par, :, :], ACT.Copy).then_inc(hi_ready, 1)

        def vector_split(dve, blk, par):
            dve.wait_ge(hi_ready, blk + 1)
            dve.tensor_tensor(w_lo[:, par, :, :], w_raw[:, par, :, :], f32(w_hi[:, par, :, :]), ALU.subtract).then_inc(split_ready, 1)

        def next_split(eng, which, first, i, u):
            nxt = first + u + 1
            if isinstance(i, int) and nxt + 2 * i >= NBLK:
                return
            if which == "scalar":
                scalar_split(eng, nxt + 2 * i, nxt % 2, nxt // 2 + i)
            else:
                vector_split(eng, nxt + 2 * i, nxt % 2)

        def three(pe, o, l_hi, l_lo, r_hi, r_lo, first, last):
            pe.matmul(o, l_hi, r_hi, start=first, stop=False)
            pe.matmul(o, l_hi, r_lo, start=False, stop=False)
            return pe.matmul(o, l_lo, r_hi, start=False, stop=last)

        def tensor_block_T(pe, blk, par, r_hi, r_lo, n, ready=None, tiles=(0, 1), root=None, order=tuple(range(KT)), last=None):
            pe.wait_ge(split_ready, blk + 1)
            for j in tiles:
                pe.wait_ge(tile_free, 2 * blk + j + 1)
                for k in order:
                    if last is not None and j == 0 and k == last[0]:
                        last[1]()
                    if ready is not None and j == 0 and (order[0] == 0 or k < order[0]):
                        wait(pe, *(ready(k) if callable(ready) else (ready[0], ready[1] + ready[2] * k + 1)))
                    w = slice(j * P, j * P + P)
                    mm = three(pe, ps[:, 2 * par + j, 0:n], w_hi[:, par, k, w], w_lo[:, par, k, w],
                               r_hi[:, k, 0:n], r_lo[:, k, 0:n], k == order[0], k == order[-1])
                mm.then_inc(tile_done, 1)
                if root is not None and j == 0:
                    tensor_root(pe, root)

        def tensor_block_N(pe, blk, par, plan):
            a_hi, a_lo = (m_hi, m_lo) if plan is MEMORY else (h_hi, h_lo)
            pe.wait_ge(split_ready, blk + 1)
            for j, parts in plan:
                pe.wait_ge(tile_free, 2 * blk + j + 1)
                for tt, c0, cn, at in parts:
                    for k in range(KT):
                        mm = three(pe, ps[:, 2 * par + j, at:at + cn], a_hi[:, k, tt * P:tt * P + P],
                                   a_lo[:, k, tt * P:tt * P + P], w_hi[:, par, k, c0:c0 + cn], w_lo[:, par, k, c0:c0 + cn],
                                   k == 0, k == KT - 1)
                mm.then_inc(tile_done, 1)

        WHOLE = [(j, [(2 * j + s, 0, BLK, s * BLK) for s in (0, 1)]) for j in (0, 1)]
        MEMORY = [(j, [(j, 0, BLK, 0)]) for j in (0, 1)]
        GATES = [(j, [(2 * j + s, 0, 48, s * 48) for s in (0, 1)]) for j in (0, 1)]
        VALUES_A = [(1, [(t, P, P, t * P) for t in range(QT)])]

        def ready(name, split=0):
            return (h_ready, NORMS[name]["h0"] + split, len(NORMS[name]["splits"]))

        def run_between(eng, between, i, u):
            if between is not None and isinstance(i, int) and 2 * i + u in between:
                between[2 * i + u](eng)

        def tensor_linear_T(pe, first, n, r_hi, r_lo, tokens=S, ready=None, root=None, between=None, order=tuple(range(KT)), last=None):
            def step(i, u):
                head = isinstance(i, int) and i + u == 0
                rooted = isinstance(i, int) and 2 * i + u == (1 if root == "mix0" else 0)
                tensor_block_T(pe, first + 2 * i + u, (first + u) % 2, r_hi, r_lo, tokens, ready if head else None,
                               root=root if rooted else None, order=order, last=last if head else None)
                run_between(pe, between, i, u)
            block_steps(pe, n, step, ahead=max(between) // 2 + 1 if between else 1 if ready else 0)

        def tensor_linear_N(pe, first, n, plan, between=None):
            def step(i, u):
                tensor_block_N(pe, first + 2 * i + u, (first + u) % 2, plan)
                run_between(pe, between, i, u)
            block_steps(pe, n, step)

        def scalar_linear(act, first, n, root=None, between=None):
            def step(i, u):
                next_split(act, "scalar", first, i, u)
                if root is not None and isinstance(i, int) and i + u == 0:
                    scalar_root(act, root)
                run_between(act, between, i, u)
            block_steps(act, n, step, ahead=max(between) // 2 + 1 if between else 1 if root else 0)

        def vector_linear(dve, first, n, evacuate, root=None, between=None):
            def step(i, u):
                next_split(dve, "vector", first, i, u)
                if root is not None and isinstance(i, int) and i + u == 0:
                    vector_root(dve, root)
                for j in (0, 1):
                    dve.wait_ge(tile_done, 2 * (first + 2 * i + u) + j + 1)
                    evacuate(i, u, j, 2 * ((first + u) % 2) + j).then_inc(tile_free, 1)
                run_between(dve, between, i, u)
            block_steps(dve, n, step, ahead=max(between) // 2 + 1 if between else 1 if root else 0)

        def scalar_residual(act, name):
            first = NORMS[name]["first"]
            for q in range(4):
                next_split(act, "scalar", first, 0, q)
                for j in (0, 1):
                    scalar_tile(act, name, 2 * q + j)

        def vector_residual(dve, name):
            first = NORMS[name]["first"]
            for q in range(4):
                next_split(dve, "vector", first, 0, q)
                for j in (0, 1):
                    t = 2 * q + j
                    dve.wait_ge(tile_done, 2 * first + t + 1)
                    dve.tensor_tensor(x[:, t, :], ps[:, 2 * ((first + q) % 2) + j, :], x[:, t, :], ALU.add).then_inc(tile_free, 1)
                    vector_tile(dve, name, t)

        def to_T(dve, dst, n=S, root=rstd):
            return lambda i, u, j, bank: dve.tensor_tensor(dst[:, 4 * i + 2 * u + j, 0:n], ps[:, bank, 0:n], root[:, 0:n], ALU.mult)

        def to_N(dve, dst):
            def evacuate(i, u, j, bank):
                return dve.tensor_tensor(dst[:, 2 * j:2 * j + 2, span(BLK * (2 * i + u), BLK)],
                                         ps[:, bank, :].rearrange("p (a b) -> p a b", a=2),
                                         rcol[:, 2 * j:2 * j + 2].unsqueeze(2).broadcast_to([P, 2, BLK]), ALU.mult)
            return evacuate

        def chunk_steps(eng, body):
            body(0)
            with eng.Fori(1, CH - 1) as c:
                body(c)
            body(CH - 1)

        def tensor_mlp(pe, m, name):
            first = b["mlp%d" % m]

            def body(c):
                start = isinstance(c, int) and c == 0
                for q in range(4):
                    head = start and q == 0
                    tensor_block_T(pe, first + 8 * c + q, (first + q) % 2, h_hi, h_lo, S, ready(name) if head else None,
                                   root=name if head else None)
                for q in range(4, 8):
                    tensor_block_T(pe, first + 8 * c + q, (first + q) % 2, o_hi, o_lo, S,
                                   (hid_ready, 8 * (CH * m + c), 1) if q == 4 else None)
            chunk_steps(pe, body)

        def scalar_mlp(act, m, name, following):
            first = b["mlp%d" % m]

            def body(c):
                for q in range(8):
                    blk = first + 8 * c + q
                    if not (isinstance(c, int) and blk + 1 >= NBLK):
                        scalar_split(act, blk + 1, (first + q + 1) % 2, (first + q + 1) // 2 + 4 * c)
                    if isinstance(c, int) and c + q == 0:
                        scalar_root(act, name)
                    for j in (0, 1):
                        t = 2 * q + j
                        n = 8 * (CH * m + c) + t
                        if q < 4:
                            act.wait_ge(tile_free, 2 * blk + j + 5)
                            act.activation(hid_buf[:, t % 2, :], hid_buf[:, t % 2, :], ACT.Square).then_inc(hid_y, 1)
                            act.wait_ge(hid_y, n + 1)
                            act.activation(o_hi[:, t, :], hid_buf[:, t % 2, :], ACT.Copy).then_inc(hid_hi, 1)
                        elif isinstance(c, int) and c == CH - 1:
                            scalar_tile(act, following, t - 8)
            chunk_steps(act, body)

        def vector_mlp(dve, m, name, following):
            first = b["mlp%d" % m]

            def body(c):
                for q in range(8):
                    blk = first + 8 * c + q
                    if not (isinstance(c, int) and blk + 1 >= NBLK):
                        vector_split(dve, blk + 1, (first + q + 1) % 2)
                    if isinstance(c, int) and c + q == 0:
                        vector_root(dve, name)
                    for j in (0, 1):
                        bank = ps[:, 2 * ((first + q) % 2) + j, :]
                        dve.wait_ge(tile_done, 2 * blk + j + 1)
                        if q >= 4:
                            t = 2 * (q - 4) + j
                            dve.tensor_tensor(x[:, t, :], bank, x[:, t, :], ALU.add).then_inc(tile_free, 1)
                            if isinstance(c, int) and c == CH - 1:
                                vector_tile(dve, following, t)
                            continue
                        t = 2 * q + j
                        n = 8 * (CH * m + c) + t
                        if not (isinstance(c, int) and c == 0 and t < 2):
                            dve.wait_ge(hid_ready, n - 1)
                        dve.scalar_tensor_tensor(out=hid_buf[:, t % 2, :], in0=bank, scalar=0.0, in1=rstd[:, :],
                                                 op0=ALU.max, op1=ALU.mult).then_inc(tile_free, 1)
                        dve.wait_ge(hid_hi, n + 1)
                        dve.tensor_tensor(o_lo[:, t, :], hid_buf[:, t % 2, :], f32(o_hi[:, t, :]), ALU.subtract).then_inc(hid_ready, 1)
            chunk_steps(dve, body)

        def pipelined(eng, iterations, units, parts, ahead=0, leave=0):
            most = max(lag for lag, _ in parts)
            ahead = min(iterations, max(ahead, -(-most // units)))

            def step(it, v):
                for lag, part in parts:
                    back, unit = divmod(v - lag, units)
                    if not isinstance(it, int) or 0 <= it + back < iterations:
                        part(it + back, unit)
            for it in range(ahead):
                for v in range(units):
                    step(it, v)
            if ahead < iterations:
                with eng.Fori(ahead, iterations) as it:
                    for v in range(units):
                        step(it, v)
            for v in range(most - leave):
                step(iterations + v // units, v % units)

        SBH = 16

        def tensor_sb(pe):
            pe.wait_ge(const_landed, 16 * len(CONSTS))
            pe.wait_ge(tile_free, 4 + 2 * b["sb_o"])

            def z(it, u):
                n = 2 * it + u
                r = slice(HD * u, HD * u + HD)
                if isinstance(it, int) and it < 2:
                    keys, queries = sb_qk[:, 8 + it, :], sb_qk[:, it, :]
                else:
                    keys, queries = sb_ks[:, :], sb_qs[:, :]
                    pe.wait_ge(b_qk, it - 1)
                wait(pe, zs_ready, n)
                for j in range(QT):
                    mm = pe.matmul(sc[:, KOFF[j]:KOFF[j] + S - P * j], keys[r, P * j:P * j + P], queries[r, P * j:S],
                                   start=True, stop=True)
                mm.then_inc(z_done, 1)

            def cum(it, u):
                n = 2 * it + u
                pe.wait_ge(sp_ready, n + 1)
                wait(pe, arg_ready, n)
                for j in range(QT):
                    for i in range(j, QT):
                        mm = pe.matmul(pt[:, KOFF[j] + P * (i - j):KOFF[j] + S - P * j], upper[:, :] if i == j else ones[:, :],
                                       spl[:, KOFF[i]:KOFF[i] + S - P * i], start=(i == j), stop=(i == QT - 1))
                mm.then_inc(cum_done, 1)

            def pv(it, u):
                n = 2 * it + u
                pe.wait_ge(a_ready, n + 1)
                pe.wait_ge(b_v, it + 1)
                wait(pe, blo_done, n)
                for j in range(QT):
                    mm = pe.matmul(ps[HD * u:HD * u + HD, 6 + u, P * j:S], sb_vs[:, j, HD * u:HD * u + HD],
                                   stick[:, u, KOFF[j]:KOFF[j] + S - P * j], start=(j == 0), stop=(j == QT - 1))
                mm.then_inc(bpv_done, 1)
            pipelined(pe, SBH // 2, 2, [(0, z), (3, pv), (1, cum)], leave=1)
            pe.wait_ge(zs_ready, SBH)
            return lambda: pv(SBH // 2 - 1, 1)

        def scalar_sb(act):
            def softplus(it, u):
                n = 2 * it + u
                act.wait_ge(nabs_ready, n + 1)
                act.activation(soft[:, :], soft[:, :], ACT.Exp).then_inc(e_ready, 1)
                act.wait_ge(e_ready, n + 1)
                act.activation(soft[:, :], soft[:, :], ACT.Ln, bias=1.0).then_inc(l_ready, 1)

            def weights(it, u):
                n = 2 * it + u
                act.wait_ge(arg_ready, n + 1)
                act.activation(stick[:, u, :], stick[:, u, :], ACT.Exp).then_inc(a_ready, 1)

            def high(it, u):
                n = 2 * it + u
                r = slice(HD * u, HD * u + HD)
                act.wait_ge(bpv_done, n + 1)
                act.activation(o_hi[r, it, :], ps[r, 6 + u, :], ACT.Copy).then_inc(bhi_done, 1)
            pipelined(act, SBH // 2, 2, [(3, high), (0, softplus), (1, weights)])

        def vector_sb(dve):
            def masked(it, u):
                n = 2 * it + u
                dve.wait_ge(z_done, n + 1)
                wait(dve, sp_ready, n)
                wait(dve, arg_ready, n - 1)
                for j in range(QT):
                    c = slice(KOFF[j], KOFF[j] + S - P * j)
                    ins = dve.scalar_tensor_tensor(out=zs[:, u, c], in0=sc[:, c], scalar=HD ** -0.5, in1=m_sb[:, 0:S - P * j],
                                                   op0=ALU.mult, op1=ALU.min)
                ins.then_inc(zs_ready, 1)
                dve.wait_ge(zs_ready, n + 1)
                dve.scalar_tensor_tensor(out=soft[:, :], in0=zs[:, u, :], scalar=-1.0, in1=zs[:, u, :], op0=ALU.mult,
                                         op1=ALU.min).then_inc(nabs_ready, 1)

            def argument(it, u):
                n = 2 * it + u
                dve.wait_ge(cum_done, n + 1)
                wait(dve, bpv_done, n - 1)
                dve.tensor_tensor(stick[:, u, :], zs[:, u, :], pt[:, 0:CW], ALU.subtract).then_inc(arg_ready, 1)

            def softplus(it, u):
                n = 2 * it + u
                dve.wait_ge(l_ready, n + 1)
                wait(dve, cum_done, n)
                dve.scalar_tensor_tensor(out=spl[:, :], in0=zs[:, u, :], scalar=0.0, in1=soft[:, :], op0=ALU.max,
                                         op1=ALU.add).then_inc(sp_ready, 1)

            def low(it, u):
                n = 2 * it + u
                r = slice(HD * u, HD * u + HD)
                dve.wait_ge(bhi_done, n + 1)
                dve.tensor_tensor(o_lo[r, it, :], ps[r, 6 + u, :], f32(o_hi[r, it, :]), ALU.subtract).then_inc(blo_done, 1)
            pipelined(dve, SBH // 2, 2, [(0, masked), (3, low), (1, argument), (0, softplus)])

        def pool_sb(pool):
            pool.wait_ge(tile_free, 4 + 2 * b["sb_o"])

            def queries_keys(p):
                if not isinstance(p, int) or p > 2:
                    pool.wait_ge(z_done, 2 * p)
                pool.tensor_copy(sb_qs[:, :], sb_qk[:, p, :])
                pool.tensor_copy(sb_ks[:, :], sb_qk[:, 8 + p, :]).then_inc(b_qk, 1)

            def pair_values(p):
                wait(pool, bpv_done, 2 * p)
                src = sb_v[:, :, bass.ds(P * p, P)] if not isinstance(p, int) else sb_v[:, :, P * p:P * p + P]
                pool.tensor_copy(sb_vs[:, :, :], src).then_inc(b_v, 1)
            pair_values(0)
            queries_keys(2)
            pair_values(1)
            with pool.Fori(3, SBH // 2) as p:
                queries_keys(p)
                pair_values(p - 1)
            pair_values(SBH // 2 - 1)

        CAUSAL_Q = [(t, QOFF[t], P * (t + 1)) for t in range(QT)]

        def scores_causal(q, k):
            return [(sc[:, QOFF[t]:QOFF[t] + P * (t + 1)], q[:, P * t:P * t + P], k[:, 0:P * (t + 1)], True, True) for t in range(QT)]

        def turns_causal(par):
            return [(pt[:, KOFF[j] + P * (t - j):KOFF[j] + P * (t - j) + P], probs[:, par, QOFF[t] + P * j:QOFF[t] + P * j + P])
                    for j in range(QT) for t in range(j, QT)]

        def values_causal(o, v, par, first, last):
            return [(o[:, P * j:S], v(j), probsT[:, par, KOFF[j]:KOFF[j] + S - P * j], first and j == 0, last and j == QT - 1)
                    for j in range(QT)]

        def nsa_units(q_rot, q_plain, k_slc, k_win, k_cmp):
            def compressed(hh):
                r = slice(NCP * hh, NCP * hh + NCP)
                return (ps[HD * (hh % 2):HD * (hh % 2) + HD, 6 + hh % 2, :], nv_cmp[r, :], cmpT[r, :], True, False)
            units = [dict(par=0, head=0, branch=2, opens=True, closes=False, bank=6, rows=slice(0, HD),
                          scores=[(sc[:, S * (hh % 2) + 2 * NCP * t + NCP * (hh // 2):S * (hh % 2) + 2 * NCP * t + NCP * (hh // 2) + NCP],
                                   q_plain[HD * (hh % 2):HD * (hh % 2) + HD, hh // 2, P * t:P * t + P],
                                   k_cmp[HD * (hh % 2):HD * (hh % 2) + HD, :], True, True) for t in range(QT) for hh in range(4)],
                          turns=[(pt[:, P * t:P * t + P], pcmp[:, P * t:P * t + P]) for t in range(QT)],
                          values=[compressed(0)])]
            for hh in range(4):
                r = slice(HD * (hh % 2), HD * (hh % 2) + HD)
                o = ps[r, 6 + hh % 2, :]
                for br, (k, v) in enumerate([(k_slc, nv_slc), (k_win, nv_win)]):
                    par = len(units) % 2
                    first = [compressed(hh)] if br == 0 and hh > 0 else []
                    units.append(dict(
                        par=par, head=hh, branch=br, opens=(br == 0 and hh > 0), closes=(br == 1), bank=6 + hh % 2, rows=r,
                        scores=scores_causal(q_rot[r, hh // 2, :], k[r, :]),
                        regions=[(t, QOFF[t], P * (t + 1), m_causal[:, S - P * (t + 1):S]) for t in range(QT)],
                        turns=turns_causal(par), copy=(P, CW),
                        values=first + values_causal(o, lambda j, v=v: v[:, j, :], par, False, br == 1)))
            return units

        SWQ = {0: 0, 1: 128, 2: 512, 3: 768}
        SWK = {0: 0, 1: 256, 2: 512, 3: 768}

        def swa_units(q, k, vals):
            units = []
            for g in range(4):
                r = slice(HD * (g % 2), HD * (g % 2) + HD)
                par = g % 2
                o = ps[r, 6 + g % 2, :]
                scores, regions, turns, values = [], [], [], []
                for t in range(QT):
                    k0 = P * max(t - 1, 0)
                    w = P * (t + 1) - k0
                    scores.append((sc[:, SWQ[t]:SWQ[t] + w], q[r, g // 2, P * t:P * t + P], k[r, k0:k0 + w], True, True))
                    regions.append((t, SWQ[t], w, m_swa[:, 2 * P - w:2 * P]))
                    for j in range(max(t - 1, 0), t + 1):
                        at = SWK[j] + P * (t - j)
                        turns.append((pt[:, at:at + P], probs[:, par, SWQ[t] + P * j - k0:SWQ[t] + P * j - k0 + P]))
                        values.append((o[:, P * t:P * t + P], vals[:, j, :], probsT[:, par, at:at + P], j == max(t - 1, 0), j == t))
                units.append(dict(par=par, head=g, branch=0, opens=True, closes=True, bank=6 + g % 2, rows=r, scores=scores,
                                  regions=regions, turns=turns, copy=(P, 7 * P), values=values))
            return units

        def diff_units(q, k):
            units = []
            for c in range(2):
                r = slice(HD * c, HD * c + HD)
                units.append(dict(par=c, head=0, branch=c, opens=(c == 0), closes=(c == 1), bank=6, rows=slice(0, P),
                                  scores=scores_causal(q[r, :], k[r, :]),
                                  regions=[(t, QOFF[t], P * (t + 1), m_causal[:, S - P * (t + 1):S]) for t in range(QT)],
                                  turns=turns_causal(c), copy=(P, CW),
                                  values=values_causal(ps[:, 6, :], lambda j: dv_s[:, j, :], c, c == 0, c == 1)))
            return units

        def cross_units(q, k, v):
            units = []
            for u in range(2):
                scores, values = [], []
                for t in range(QT):
                    for kc in range(2):
                        scores.append((sc[:, MEM * t:MEM * t + MEM], q[:, 2 * u + kc, P * t:P * t + P], k[:, 2 * u + kc, :],
                                       kc == 0, kc == 1))
                for mt in range(2):
                    for j in range(2):
                        values.append((ps[:, 6 + mt, :], v[:, j, MEM * u + P * mt:MEM * u + P * mt + P],
                                       probsT[:, u, S * j:S * j + S], j == 0, j == 1))
                units.append(dict(par=u, head=u, branch=0, opens=True, closes=True, bank=None, rows=slice(0, P), scores=scores,
                                  regions=[(t, MEM * t, MEM, None) for t in range(QT)],
                                  turns=[(pt[:, S * j + P * t:S * j + P * t + P], probs[:, u, MEM * t + P * j:MEM * t + P * j + P])
                                         for j in range(2) for t in range(QT)],
                                  copy=(P, 2 * S), values=values))
            return units

        rows_of = lambda ap: ap.rearrange("p (a b) -> p a b", b=NCP)
        cmp4 = lambda ap: ap.rearrange("p (a b) -> p a b", a=QT)

        def scalar_cmp_copy(act, a, it, n):
            act.wait_ge(t_done, n + 1)
            wait(act, pv_done, n - 1)
            act.activation(cmpT[:, :], pt[:, 0:S], ACT.Copy).then_inc(pt_copied, 1)

        def scalar_cmp_exp(act, it, n):
            act.wait_ge(nm_ready, n + 1)
            act.activation(pcmp[:, :], pcmp[:, :], ACT.Exp, scale=HD ** -0.5).then_inc(p_ready, 1)

        def vector_cmp_largest(dve, it, n):
            pc = pcmp[:, :]
            for odd in (0, 1):
                s = sc[:, S * odd:S * odd + 8 * NCP].rearrange("p (t h n) -> p t h n", t=QT, h=2)
                d = pc.rearrange("p (t h o n) -> p t h o n", t=QT, h=2, o=2)[:, :, :, odd, :]
                ins = dve.tensor_tensor(d, s, m_cmp[:, :, :].unsqueeze(2).broadcast_to([P, QT, 2, NCP]), ALU.add)
            ins.then_inc(mx_ready, 1)
            dve.wait_ge(mx_ready, n + 1)
            dve.tensor_reduce(cstat[:, 0, :], rows_of(pc), AXL.X, ALU.max).then_inc(cs_max, 1)
            dve.wait_ge(cs_max, it + 1)
            dve.tensor_tensor(rows_of(pc), rows_of(pc), cstat[:, 0, :].unsqueeze(2).broadcast_to([P, 16, NCP]),
                              ALU.subtract).then_inc(nm_ready, 1)

        def vector_cmp_normal(dve, it, n):
            pc = pcmp[:, :]
            dve.wait_ge(p_ready, n + 1)
            dve.tensor_reduce(cstat[:, 1, :], rows_of(pc), AXL.X, ALU.add).then_inc(cs_sum, 1)
            g = gates[:, :, span(4 * it, 4)]
            dve.tensor_tensor(cmp4(cstat[:, 2, :]), g, anyv[:, :].unsqueeze(2).broadcast_to([P, QT, 4]), ALU.mult).then_inc(cs_gate, 1)
            dve.wait_ge(cs_sum, it + 1)
            dve.reciprocal(cstat[:, 1, :], cstat[:, 1, :]).then_inc(rc_ready, 1)
            dve.wait_ge(rc_ready, n + 1)
            dve.wait_ge(cs_gate, it + 1)
            dve.tensor_tensor(cstat[:, 3, :], cstat[:, 1, :], cstat[:, 2, :], ALU.mult).then_inc(cs_fac, 1)
            dve.wait_ge(cs_fac, it + 1)
            dve.tensor_tensor(rows_of(pc), rows_of(pc), cstat[:, 3, :].unsqueeze(2).broadcast_to([P, 16, NCP]),
                              ALU.mult).then_inc(pn_ready, 1)

        staged = dict(nsa=nsa_units(nq_rot[:, :, :], nq_plain[:, :, :], nk_slc[:, :], nk_win[:, :], nk_cmp[:, :]),
                      diff=diff_units(dq_s[:, :], dk_s[:, :]))
        direct = dict(nsa=[nsa_units(q_rot[:, 0:2, :], q_plain[:, 0:2, :], k_slc[:, 0, :], k_win[:, 0, :], k_cmp[:, 0, :])],
                      swa=[swa_units(inp[:, 2 * k:2 * k + 2, :], ka_dup[:, k, :], va[:, :, HD * k:HD * k + HD]) for k in range(2)],
                      diff=[diff_units(inp[:, 4 + h, :], inp[:, 8 + h, :]) for h in range(2)],
                      cross=[cross_units(c_q[:, 4 * i:4 * i + 4, :], c_k[:, 4 * i:4 * i + 4, :], c_v[:, :, 512 * i:512 * i + 512])
                             for i in range(2)])
        for name in ("swa", "cross"):
            staged[name] = direct[name][0]
        def tensor_dsum(pe, it, v):
            if v % 2 == 0:
                h = 2 * it + v // 2
                pe.wait_ge(dsq, h + 1)
                wait(pe, dstd, h)
                pe.matmul(ps[:, 5, :], ones[:, :], d_sq[:, :], start=True, stop=True).then_inc(dsum, 1)

        def scalar_dsquare(act, it, v):
            if v % 2 == 0:
                h = 2 * it + v // 2
                act.wait_ge(olo_done, ATT["diff"]["o0"] + h + 1)
                wait(act, dsum, h)
                act.activation(d_sq[:, :], od[:, h, :], ACT.Square).then_inc(dsq, 1)

        def scalar_dstd(act, it, v):
            if v % 2 == 0:
                h = 2 * it + v // 2
                act.wait_ge(dsum, h + 1)
                wait(act, dy, h)
                act.activation(rstd[:, :], ps[:, 5, :], ACT.Sqrt, bias=eps_c[:, 0:1], scale=1.0 / P).then_inc(dstd, 1)

        def vector_dnorm(dve, it, v):
            if v % 2 == 0:
                h = 2 * it + v // 2
                dve.wait_ge(dstd, h + 1)
                dve.reciprocal(rstd[:, :], rstd[:, :]).then_inc(drstd, 1)
                dve.wait_ge(drstd, h + 1)
                wait(dve, dlo, h)
                dve.scalar_tensor_tensor(out=d_y[:, :], in0=od[:, h, :], scalar=gdiff[:, 0:1], in1=rstd[:, :],
                                           op0=ALU.mult, op1=ALU.mult).then_inc(dy, 1)

        def scalar_dhigh(act, it, v):
            if v % 2 == 0:
                h = 2 * it + v // 2
                act.wait_ge(dy, h + 1)
                act.activation(o_hi[:, 4 + h, :], d_y[:, :], ACT.Copy).then_inc(dhi, 1)

        def vector_dlow(dve, it, v):
            if v % 2 == 0:
                h = 2 * it + v // 2
                dve.wait_ge(dhi, h + 1)
                dve.tensor_tensor(o_lo[:, 4 + h, :], d_y[:, :], f32(o_hi[:, 4 + h, :]), ALU.subtract).then_inc(dlo, 1)

        ATT = {}
        n0 = o0 = i0 = v0 = 0
        for name, its, scale in [("nsa", 4, HD ** -0.5), ("diff", 4, HD ** -0.5), ("swa", 2, HD ** -0.5), ("cross", 2, MEM ** -0.5)]:
            units = staged[name]
            closes = sum(u["closes"] for u in units)
            parts = {0: 1, 1: 3, 2: 4} if name == "nsa" else {0: 1}
            ATT[name] = dict(parts=parts, n0=n0, o0=o0, i0=i0, v0=v0, its=its, units=units, scale=scale, closes=closes, direct=direct[name])
            n0 += its * len(units)
            o0 += its * closes
            i0 += max(parts.values()) * (its - len(direct[name]))
            v0 += 0 if name in ("swa", "cross") else its

        def unit_no(a, it, v):
            return a["n0"] + len(a["units"]) * it + v

        def output_no(a, it, v):
            return a["o0"] + a["closes"] * it + sum(u["closes"] for u in a["units"][:v])

        def tensor_attention(pe, name):
            a = ATT[name]
            U = a["units"]

            def scores(it, v):
                ahead = len(a["direct"])
                in_place = isinstance(it, int) and it < ahead
                if v in a["parts"] and not in_place:
                    pe.wait_ge(st_qk, a["i0"] + max(a["parts"].values()) * (it - ahead) + a["parts"][v])
                wait(pe, mx_ready, unit_no(a, it, v))
                for o, l, r, first, last in (a["direct"][it] if in_place else U)[v]["scores"]:
                    mm = pe.matmul(o, l, r, start=first, stop=last)
                mm.then_inc(s_done, 1)

            def turn(it, v):
                pe.wait_ge(pn_ready, unit_no(a, it, v) + 1)
                wait(pe, pt_copied, unit_no(a, it, v))
                for o, i in U[v]["turns"]:
                    mm = pe.transpose(o, i, ident[:, :])
                mm.then_inc(t_done, 1)

            def values(it, v):
                pe.wait_ge(pt_copied, unit_no(a, it, v) + 1)
                if v == 0 and name not in ("swa", "cross"):
                    pe.wait_ge(st_v, a["v0"] + it + 1)
                if U[v]["opens"]:
                    back = 1 if name in ("nsa", "swa") and not (name == "swa" and isinstance(it, int) and it + v == 0) else 0
                    wait(pe, olo_done, output_no(a, it, v) - back)
                for o, l, r, first, last in (a["direct"][it] if name in ("swa", "cross") else U)[v]["values"]:
                    mm = pe.matmul(o, l, r, start=first, stop=last)
                mm.then_inc(pv_done, 1)
            more = [(1, lambda it, v: tensor_dsum(pe, it, v))] if name == "swa" else []
            pipelined(pe, a["its"], len(U), [(2, turn), (0, scores), (3, values)] + more, ahead=len(a["direct"]), leave=1)
            pe.wait_ge(mx_ready, unit_no(a, a["its"], 0))
            return lambda: values(a["its"] - 1, len(U) - 1)

        def scalar_attention(act, name):
            a = ATT[name]
            U = a["units"]

            def copy(it, v):
                n = unit_no(a, it, v)
                if name == "nsa" and v == 0:
                    scalar_cmp_copy(act, a, it, n)
                    return
                rows, width = U[v]["copy"]
                act.wait_ge(t_done, n + 1)
                wait(act, pv_done, n - 1)
                act.activation(probsT[0:rows, U[v]["par"], 0:width], pt[0:rows, 0:width], ACT.Copy).then_inc(pt_copied, 1)

            def expo(it, v):
                n = unit_no(a, it, v)
                par = U[v]["par"]
                if name == "nsa" and v == 0:
                    scalar_cmp_exp(act, it, n)
                    return
                act.wait_ge(nm_ready, n + 1)
                if name == "swa":
                    h = 4 * it + U[v]["head"]
                    sk = sinks[:, bass.ds(h, 1)] if not isinstance(h, int) else sinks[:, h:h + 1]
                    for t in range(QT):
                        ins = act.activation(stat_sink[:, par, t:t + 1], stat_nm[:, par, t:t + 1], ACT.Exp, bias=sk)
                for t, at, w, mask in U[v]["regions"]:
                    ins = act.activation(probs[:, par, at:at + w], probs[:, par, at:at + w], ACT.Exp,
                                         bias=stat_nm[:, par, t:t + 1], accum_out=stat_sum[:, par, t:t + 1])
                ins.then_inc(p_ready, 1)

            def high(it, v):
                if not U[v]["closes"]:
                    return
                act.wait_ge(pv_done, unit_no(a, it, v) + 1)
                r = U[v]["rows"]
                if name == "nsa":
                    ins = act.activation(o_hi[r, 2 * it + U[v]["head"] // 2, :], ps[r, U[v]["bank"], :], ACT.Copy)
                elif name == "swa":
                    ins = act.activation(o_hi[r, 2 * it + U[v]["head"] // 2, :], ps[r, U[v]["bank"], :], ACT.Copy)
                elif name == "diff":
                    ins = act.activation(od[:, it, 0:S // 2], ps[:, 6, 0:S // 2], ACT.Copy)
                else:
                    for mt in range(2):
                        ins = act.activation(o_hi[:, 4 * it + 2 * v + mt, :], ps[:, 6 + mt, :], ACT.Copy)
                ins.then_inc(ohi_done, 1)
            more = [(3, lambda it, v: scalar_dhigh(act, it, v)), (0, lambda it, v: scalar_dsquare(act, it, v)),
                    (2, lambda it, v: scalar_dstd(act, it, v))] if name == "swa" else []
            pipelined(act, a["its"], len(U), [(2, copy), (0, expo), (3, high)] + more, ahead=len(a["direct"]))

        def vector_attention(dve, name):
            a = ATT[name]
            U = a["units"]

            def largest(it, v):
                n = unit_no(a, it, v)
                par = U[v]["par"]
                dve.wait_ge(s_done, n + 1)
                wait(dve, t_done, n - 1)
                if name == "nsa" and v == 0:
                    vector_cmp_largest(dve, it, n)
                    return
                dve.sem_inc(begun)
                for t, at, w, mask in U[v]["regions"]:
                    if mask is None:
                        dve.tensor_scalar(probs[:, par, at:at + w], sc[:, at:at + w], a["scale"], None, ALU.mult)
                        ins = dve.tensor_reduce(stat_max[:, par, t:t + 1], sc[:, at:at + w], AXL.X, ALU.max)
                    else:
                        ins = dve.tensor_tensor_reduce(probs[:, par, at:at + w], sc[:, at:at + w], mask, a["scale"], -BIG,
                                                       ALU.add, ALU.max, stat_max[:, par, t:t + 1])
                ins.then_inc(mx_ready, 1)
                dve.wait_ge(mx_ready, n + 1)
                if name == "swa":
                    h = 4 * it + U[v]["head"]
                    sk = nsink[:, bass.ds(h, 1)] if not isinstance(h, int) else nsink[:, h:h + 1]
                    dve.tensor_scalar(stat_nm[:, par, :], stat_max[:, par, :], -1.0, sk, ALU.mult, ALU.min).then_inc(nm_ready, 1)
                else:
                    dve.tensor_scalar(stat_nm[:, par, :], stat_max[:, par, :], -a["scale"] if name == "cross" else -1.0, None,
                                      ALU.mult).then_inc(nm_ready, 1)

            def normal(it, v):
                n = unit_no(a, it, v)
                par = U[v]["par"]
                if name == "nsa" and v == 0:
                    vector_cmp_normal(dve, it, n)
                    return
                dve.wait_ge(p_ready, n + 1)
                total = stat_sum
                if name == "swa":
                    dve.tensor_tensor(stat_sum[:, par, :], stat_sum[:, par, :], stat_sink[:, par, :], ALU.add).then_inc(den_ready, 1)
                    dve.wait_ge(den_ready, n - a["n0"] + 1)
                dve.reciprocal(stat_rc[:, par, :], total[:, par, :]).then_inc(rc_ready, 1)
                dve.wait_ge(rc_ready, n + 1)
                fac = stat_fac
                if name == "nsa":
                    c = 16 * (U[v]["branch"] + 1) + 4 * it + U[v]["head"]
                    g = gates[:, :, bass.ds(c, 1)] if not isinstance(c, int) else gates[:, :, c:c + 1]
                    dve.tensor_tensor(stat_fac[:, par, :], stat_rc[:, par, :], g.rearrange("p a b -> p (a b)"), ALU.mult).then_inc(fac_ready, 1)
                    fn = 8 * it + v
                elif name == "diff":
                    dve.tensor_scalar(stat_fac[:, par, :], stat_rc[:, par, :], neglam[:, 0:1] if v == 1 else 1.0, None,
                                      ALU.mult).then_inc(fac_ready, 1)
                    fn = n - a["n0"] + 33
                else:
                    fac = stat_rc
                    fn = None
                if fn is not None:
                    dve.wait_ge(fac_ready, fn)
                for t, at, w, mask in U[v]["regions"]:
                    ins = dve.tensor_scalar(probs[:, par, at:at + w], probs[:, par, at:at + w], fac[:, par, t:t + 1], None, ALU.mult)
                ins.then_inc(pn_ready, 1)

            def low(it, v):
                if not U[v]["closes"]:
                    return
                r = U[v]["rows"]
                dve.wait_ge(ohi_done, output_no(a, it, v) + 1)
                if name in ("nsa", "swa"):
                    t = 2 * it + U[v]["head"] // 2
                    ins = dve.tensor_tensor(o_lo[r, t, :], ps[r, U[v]["bank"], :], f32(o_hi[r, t, :]), ALU.subtract)
                elif name == "diff":
                    ins = dve.tensor_copy(od[:, it, S // 2:S], ps[:, 6, S // 2:S])
                else:
                    for mt in range(2):
                        t = 4 * it + 2 * v + mt
                        ins = dve.tensor_tensor(o_lo[:, t, :], ps[:, 6 + mt, :], f32(o_hi[:, t, :]), ALU.subtract)
                ins.then_inc(olo_done, 1)
            more = [(3, lambda it, v: vector_dlow(dve, it, v)), (2, lambda it, v: vector_dnorm(dve, it, v))] if name == "swa" else []
            pipelined(dve, a["its"], len(U), [(1, normal), (0, largest), (3, low)] + more, ahead=len(a["direct"]))

        cs_max, cs_sum, cs_gate, cs_fac = (sem("cs_" + n) for n in ("max", "sum", "gate", "fac"))
        begun = sem("begun")

        def pool_attention(pool, name, first, qk, vals):
            a = ATT[name]
            for s, value in first:
                pool.wait_ge(s, value)

            ahead = len(a["direct"])

            def queries_keys(it):
                for used, copies in qk(it):
                    if not isinstance(it, int) or it > ahead:
                        pool.wait_ge(s_done, a["n0"] + len(a["units"]) * (it - 1) + used)
                    for d, s in copies:
                        ins = pool.tensor_copy(d, s)
                    ins.then_inc(st_qk, 1)

            def turn_values(it):
                wait(pool, pv_done, a["n0"] + len(a["units"]) * it)
                for d, s in vals(it):
                    ins = pool.tensor_copy(d, s)
                ins.then_inc(st_v, 1)
            late = 1 if len(a["units"]) < 3 else 0
            turn_values(0)
            queries_keys(ahead)
            turn_values(ahead - late)
            if ahead + 1 < a["its"]:
                with pool.Fori(ahead + 1, a["its"]) as it:
                    queries_keys(it)
                    turn_values(it - late)
            if late:
                turn_values(a["its"] - 1)

        def pool_nsa(pool):
            pool_attention(pool, "nsa", [(tile_free, 4 + 2 * b["nsa_o"]), (rope_ready, 12), (g_ready, 1), (dup_k, 256), (ccmp_done, 2)],
                           lambda g: [(1, [(nq_plain[:, :, :], q_plain[:, span(2 * g, 2), :]), (nk_cmp[:, :], k_cmp[:, g, :])]),
                                      (5, [(nq_rot[:, 0, :], q_rot[:, 2 * g, :])]), (8, [(nk_slc[:, :], k_slc[:, g, :])]),
                                      (9, [(nk_win[:, :], k_win[:, g, :]), (nq_rot[:, 1, :], q_rot[:, 2 * g + 1, :])])],
                           lambda g: [(nv_cmp[:, :], v_cmp[:, g, :]), (nv_slc[:, :, :], v_slc[:, :, span(HD * g, HD)]),
                                      (nv_win[:, :, :], v_win[:, :, span(HD * g, HD)])])

        def pool_diff(pool):
            pool_attention(pool, "diff", [(tile_free, 4 + 2 * b["out"]), (rope_ready, 25)],
                           lambda h: [(2, [(dq_s[:, :], inp[:, 4 + h, :]), (dk_s[:, :], inp[:, 8 + h, :])])],
                           lambda h: [(dv_s[:, :, :], vd[:, :, span(P * h, P)])])

        ROPES = [(rot1, kv_nat[:, 4 + t, :], kv_nat[:, 4 + t, :]) for t in range(4)]
        ROPES += [(rot1, q_plain[:, t, :], q_rot[:, t, :]) for t in range(KT)]
        ROPES += [(rot2, inp[:, t, :], inp[:, t, :]) for t in (0, 1, 2, 3, 4, 5, 6, 7, 8, 9, 12, 10, 11)]
        KEYS_A = 4 + KT + 11

        def rope_bank(k):
            return 4 + k % 2 if k < 4 + KT else 4 + k % 4

        def tensor_rope(pe, first, n):
            for k in range(first, first + n):
                rot, src, dst = ROPES[k]
                wait(pe, rope_b, k - (1 if k < 4 + KT else 3))
                pe.matmul(ps[:, rope_bank(k), :], rot[:, :], src, start=True, stop=True).then_inc(rope_mm, 1)

        def vector_rope(dve, first, n):
            for k in range(first, first + n):
                rot, src, dst = ROPES[k]
                wait(dve, rope_ready, k)
                dve.tensor_tensor(rope_t[:, 0, :], src, cosT[:, :], ALU.mult).then_inc(rope_a, 1)
                dve.wait_ge(rope_mm, k + 1)
                dve.tensor_tensor(rope_t[:, 1, :], ps[:, rope_bank(k), :], sinT[:, :], ALU.mult).then_inc(rope_b, 1)
                dve.wait_ge(rope_a, k + 1)
                dve.wait_ge(rope_b, k + 1)
                dve.tensor_tensor(dst, rope_t[:, 0, :], rope_t[:, 1, :], ALU.add).then_inc(rope_ready, 1)

        TC = 4 * NCMP

        def tensor_compress(pe):
            for c in range(2):
                for half in range(2):
                    blk = b["cmp"] + 2 * c + half
                    pe.wait_ge(b_split, c + 1)
                    pe.wait_ge(split_ready, blk + 1)
                    pe.wait_ge(tile_free, 4 + 2 * b["cmp"])
                    for k in range(KT):
                        r = slice((16 * c + 8 * half + k) * TC, (16 * c + 8 * half + k + 1) * TC)
                        mm = three(pe, ps[0:TC, 2 * (b["cmp"] % 2) + c, 0:BLK], bh[:, r], bl[:, r], w_hi[:, blk % 2, k, :],
                                   w_lo[:, blk % 2, k, :], half == 0 and k == 0, half == 1 and k == KT - 1)
                    mm.then_inc(tile_done, 2)

        def tensor_turn_hidden(pe):
            pe.wait_ge(cgel, 7)
            for m in range(4):
                mm = pe.transpose(ps[:, 6, TC * m:TC * m + TC], cwork[0:TC, P * m:P * m + P], ident[0:TC, 0:TC])
            mm.then_inc(cturned, 1)

        def tensor_compressed(pe):
            pe.wait_ge(cgel, 8)
            for rows in (slice(0, HD), slice(HD, P)):
                for m in range(2):
                    pe.matmul(ps[rows, 7, 0:TC], w2c[:, 0, m, :], cact[:, m, :], start=(m == 0), stop=(m == 1))
            for g in range(4):
                for m in range(2):
                    mm = pe.matmul(ps[:, 6, HD * g:HD * g + HD], cval[:, m, g, :, :].rearrange("p a b -> p (a b)"),
                                   w2c[:, 1, m, :], start=(m == 0), stop=(m == 1))
            mm.then_inc(ccmp, 1)

        bh = o_hi[:, :, :].rearrange("p a b -> p (a b)")
        bl = o_lo[:, :, :].rearrange("p a b -> p (a b)")

        def pool_compress(pool):
            pool.wait_ge(tile_free, 4 + 2 * (b["kv"] + 2))
            pool.memset(k_cmp[:, :, :], 0.0).then_inc(half_ready, 1)
            pool.memset(e_cmp[:, :, :, S - 1:S], 0.0).then_inc(half_ready, 1)
            pool.wait_ge(half_ready, 2)
            for c in range(2):
                for g in range(4):
                    src = kv_nat[HD * (g % 2):HD * (g % 2) + HD, 2 * c + g // 2, :]
                    pool.dma_start(e_cmp[0:HD, c, g, :], src).then_inc(shifted, 16)
                    pool.dma_start(e_cmp[HD:P, c, g, 0:S - 1], src[:, 1:S]).then_inc(shifted, 16)
            pool.wait_ge(shifted, 256)
            for c in range(2):
                wait(pool, b_split, c)
                for g in range(4):
                    e = e_cmp[:, c, g, 0:16 * 32].rearrange("p (n j l) -> p j n l", j=8, l=2)
                    for half in range(2):
                        n = slice(half, half + NCMP)
                        pool.tensor_tensor(b_raw[:, 8 * half:8 * half + 8, g, :], e[:, :, n, 0],
                                           cpos[:, c, 8 * half:8 * half + 8].unsqueeze(2).broadcast_to([P, 8, NCMP]),
                                           ALU.add).then_inc(b_added, 1)
            pool.wait_ge(rope_ready, 4)
            pool.wait_ge(b_split, 2)
            for dst, t0 in ((k_slc, 4), (k_win, 6)):
                for g in range(4):
                    for half in range(2):
                        pool.dma_start(dst[HD * half:HD * half + HD, g, :],
                                       kv_nat[HD * (g % 2):HD * (g % 2) + HD, t0 + g // 2, :]).then_inc(dup_k, 16)

        raw_rows = b_raw[:, :, :, :].rearrange("p a b c -> p (a b c)")

        def scalar_rows(c):
            def high(act):
                act.wait_ge(b_added, 8 * (c + 1))
                act.wait_ge(tile_done, 2 * b["kv"])
                act.activation(bh[:, 16 * TC * c:16 * TC * (c + 1)], raw_rows, ACT.Copy).then_inc(b_hi, 1)
            return high

        def vector_rows(c):
            def low(dve):
                dve.wait_ge(b_hi, c + 1)
                dve.tensor_tensor(bl[:, 16 * TC * c:16 * TC * (c + 1)], raw_rows, f32(bh[:, 16 * TC * c:16 * TC * (c + 1)]),
                                  ALU.subtract).then_inc(b_split, 1)
            return low

        def scalar_compress(act):
            for q in range(4):
                next_split(act, "scalar", b["cmp"], 0, q)
                if q == 3:
                    scalar_resplit(act)

        def vector_compress(dve):
            for q in range(4):
                next_split(dve, "vector", b["cmp"], 0, q)
                c = q // 2
                if q % 2:
                    dve.wait_ge(tile_done, 2 * (b["cmp"] + q + 1))
                    dve.tensor_copy(cpre[0:TC, BLK * c:BLK * c + BLK], ps[0:TC, 2 * (b["cmp"] % 2) + c, 0:BLK]).then_inc(tile_free, 4)
                if q == 3:
                    vector_resplit(dve)

        hu, hw, he = cpre[0:TC, :], cwork[0:TC, :], cexpb[0:TC, :]

        def vector_gelu_argument(dve):
            dve.wait_ge(tile_free, 4 + 2 * b["q"])
            dve.tensor_tensor(hw, hu, hu, ALU.mult).then_inc(cgel, 1)
            dve.wait_ge(cgel, 1)
            dve.tensor_scalar(hw, hw, 0.044715, 1.0, ALU.mult, ALU.add).then_inc(cgel, 1)
            dve.wait_ge(cgel, 2)
            dve.tensor_tensor(he, hw, hu, ALU.mult).then_inc(cgel, 1)
            dve.wait_ge(cgel, 3)
            dve.tensor_scalar(he, he, -2.0 * 0.7978845608028654, EXP_MOST, ALU.mult, ALU.min).then_inc(cgel, 1)

        def scalar_gelu(act):
            act.wait_ge(cgel, 4)
            act.activation(he, he, ACT.Exp).then_inc(cexp, 1)

        def vector_gelu(dve):
            dve.wait_ge(cexp, 1)
            dve.tensor_scalar(he, he, 1.0, None, ALU.add).then_inc(cgel, 1)
            dve.wait_ge(cgel, 5)
            dve.reciprocal(he, he).then_inc(cgel, 1)
            dve.wait_ge(cgel, 6)
            dve.tensor_tensor(hw, he, hu, ALU.mult).then_inc(cgel, 1)

        def vector_turned(dve):
            dve.memset(cval[:, :, :, :, NCMP:NCP], 0.0)
            dve.wait_ge(cturned, 1)
            dve.tensor_copy(cact[:, :, :], ps[:, 6, 0:2 * TC].rearrange("p (m n) -> p m n", m=2))
            for m in range(2):
                four = ps[:, 6, TC * (2 + m):TC * (3 + m)].rearrange("p (g n) -> p g n", g=4).unsqueeze(2).broadcast_to([P, 4, 4, NCMP])
                ins = dve.tensor_copy(cval[:, m, :, :, 0:NCMP], four)
            ins.then_inc(cgel, 1)

        def vector_compressed(dve):
            dve.wait_ge(ccmp, 1)
            dve.tensor_copy(k_cmp[:, :, 0:NCMP], ps[:, 7, 0:TC].rearrange("p (g n) -> p g n", g=4)).then_inc(ccmp_done, 1)
            dve.tensor_copy(v_cmp[:, :, :], ps[:, 6, 0:4 * HD].rearrange("p (g n) -> p g n", g=4)).then_inc(ccmp_done, 1)

        def vector_trig(dve, table):
            done = [10 * table]

            def link(ins):
                done[0] += 1
                ins.then_inc(trig_v, 1)
                dve.wait_ge(trig_v, done[0])
            ang, n = rope_t[:, 0, :], rope_t[:, 1, :]
            if table == 0:
                dve.wait_ge(pos_landed, 16)
                link(dve.tensor_copy(n, rope_i[:, :]))
                link(dve.tensor_scalar(ang, n, invf[:, 0:1], None, ALU.mult))
            for shift, add, dst in [((0.0, 0.0, sinT), (0.25, TWO_PI / 4, cosT))[table]]:
                link(dve.tensor_scalar(n, ang, 1.0 / TWO_PI, shift, ALU.mult, ALU.add))
                link(dve.tensor_scalar(n, n, MAGIC, None, ALU.add))
                link(dve.tensor_scalar(n, n, -MAGIC, None, ALU.add))
                link(dve.scalar_tensor_tensor(out=dst[:, :], in0=n, scalar=-TP1, in1=ang, op0=ALU.mult, op1=ALU.add))
                link(dve.scalar_tensor_tensor(out=dst[:, :], in0=n, scalar=-TP2, in1=dst[:, :], op0=ALU.mult, op1=ALU.add))
                link(dve.scalar_tensor_tensor(out=dst[:, :], in0=n, scalar=-TP3, in1=dst[:, :], op0=ALU.mult, op1=ALU.add))
                link(dve.tensor_scalar(dst[:, :], dst[:, :], add, PI_SAFE, ALU.add, ALU.min))
                link(dve.tensor_scalar(dst[:, :], dst[:, :], -PI_SAFE, None, ALU.max))

        def scalar_trig(act, table):
            act.wait_ge(trig_v, 10 + 8 * table)
            t = (sinT, cosT)[table]
            act.activation(t[:, :], t[:, :], ACT.Sin).then_inc(trig_a, 1)

        FIRST_CONSTS = [("gains", gain), ("eps", eps_c), ("ones", ones)]
        CONSTS = [("m_sb", m_sb), ("m_causal", m_causal), ("m_swa", m_swa), ("m_cmp", m_cmp), ("ident", ident),
                  ("upper", upper), ("rot1", rot1), ("rot2", rot2), ("cos1", cosT), ("sin1", sinT),
                  ("gate_b", gate_b), ("sinks", sinks), ("cpos", cpos), ("w2c", w2c), ("anyv", anyv), ("invf", invf),
                  ("gdiff", gdiff), ("lamw", lamw)]

        def full(t):
            return t[tuple(slice(None) for _ in t.shape)]

        def vector_consts(dve):
            dve.wait_ge(const_landed, 16 * len(CONSTS))
            for k in range(2):
                dve.tensor_tensor_reduce(lamp[:, :], lamw[:, 2 * k, :], lamw[:, 2 * k + 1, :], 1.0, 0.0, ALU.mult, ALU.add,
                                         lams[:, k:k + 1]).then_inc(lam_s, 1)
                dve.wait_ge(lam_s, k + 1)
            dve.wait_ge(lam_e, 1)
            dve.tensor_tensor(lams[:, 4:5], lams[:, 3:4], lams[:, 2:3], ALU.subtract).then_inc(lam_s, 1)
            dve.wait_ge(lam_s, 3)
            dve.tensor_scalar(neglam[:, :], lams[:, 4:5], -LAM_INIT, None, ALU.add).then_inc(lam_s, 1)
            dve.tensor_scalar(nsink[:, :], sinks[:, :], -1.0, None, ALU.mult).then_inc(lam_s, 1)
            dve.tensor_scalar(gdiff[:, :], gdiff[:, :], 1.0 - LAM_INIT, None, ALU.mult).then_inc(lam_s, 1)
            dve.tensor_tensor(gain12[:, :], g_of("final1"), g_of("mix2"), ALU.mult).then_inc(lam_s, 1)
            dve.wait_ge(lam_s, 7)
            dve.engine_nop().then_inc(consts_ready, 1)

        def scalar_consts(act):
            act.wait_ge(lam_s, 2)
            act.activation(lams[:, 2:4], lams[:, 0:2], ACT.Exp).then_inc(lam_e, 1)

        def vector_gates(dve):
            gb = gate_b[:, :].unsqueeze(1).broadcast_to([P, QT, 48])
            blk = b["gate"]
            next_split(dve, "vector", blk, 0, 0)
            for j in (0, 1):
                dve.wait_ge(tile_done, 2 * blk + j + 1)
                dve.tensor_tensor(gates[:, 2 * j:2 * j + 2, :], ps[:, 2 * (blk % 2) + j, 0:96].rearrange("p (a b) -> p a b", a=2),
                                  rcol[:, 2 * j:2 * j + 2].unsqueeze(2).broadcast_to([P, 2, 48]), ALU.mult).then_inc(tile_free, 1)
            dve.wait_ge(tile_free, 4 + 2 * (blk + 1))
            dve.tensor_tensor(gates[:, :, :], gates[:, :, :], gb, ALU.add).then_inc(gsum, 1)
            dve.wait_ge(gsum, 1)
            dve.tensor_scalar(gates[:, :, :], gates[:, :, :], -1.0, EXP_MOST, ALU.mult, ALU.min).then_inc(gsum, 1)
            vector_rope(dve, 4 + 6, 2)
            dve.wait_ge(gexp, 1)
            dve.tensor_scalar(gates[:, :, :], gates[:, :, :], 1.0, None, ALU.add).then_inc(gsum, 1)
            dve.wait_ge(gsum, 3)
            dve.reciprocal(gates[:, :, :], gates[:, :, :]).then_inc(g_ready, 1)

        def scalar_gates(act):
            next_split(act, "scalar", b["gate"], 0, 0)
            act.wait_ge(gsum, 2)
            act.activation(gates[:, :, :], gates[:, :, :], ACT.Exp).then_inc(gexp, 1)

        block = ctx.enter_context(nc.Block())

        @block.sync
        def _(sp):
            sp.dma_start(w_raw[:, 0, :, :], dram["wstream"][0]).then_inc(raw_landed[0], 16)
            for i in range(4):
                sp.dma_start(x[:, 2 * i:2 * i + 2, :], dram["xT"][:, 2 * i:2 * i + 2, :]).then_inc(x_landed[i], 16)
            sp.dma_start(w_raw[:, 1, :, :], dram["wstream"][1]).then_inc(raw_landed[1], 16)
            for name, t in CONSTS:
                sp.dma_start(full(t), dram[name]).then_inc(const_landed, 16)
            with sp.Fori(1, NBLK // 2) as i:
                for u in (0, 1):
                    sp.wait_ge(split_ready, 2 * i + u - 1)
                    sp.dma_start(w_raw[:, u, :, :], dram["wstream"][2 * i + u]).then_inc(raw_landed[u], 16)
            for t in range(KT):
                sp.wait_ge(xn_ready, KT + t + 1)
                sp.dma_start(out[:, t, :], x[:, t, :]).then_inc(out_stored, 16)
            sp.wait_ge(out_stored, 16 * KT)

        @block.gpsimd
        def _(pool):
            pool.wait_ge(const_landed, 16 * len(CONSTS))
            pool_sb(pool)
            pool_compress(pool)
            pool_nsa(pool)
            pool.wait_ge(tile_free, 4 + 2 * b["mlp1"])
            pool.wait_ge(xn_ready, KT)
            pool.dma_start(rope_i[:, :], dram["positions"]).then_inc(pos_landed, 16)
            pool.wait_ge(rope_ready, KEYS_A)
            for k in range(2):
                for half in range(2):
                    pool.dma_start(ka_dup[HD * half:HD * half + HD, k, :], inp[HD * k:HD * k + HD, 12, :]).then_inc(dup_a, 16)
            pool_diff(pool)
            pool.wait_ge(pv_done, ATT["cross"]["n0"])
            pool.wait_ge(ohi_done, ATT["cross"]["o0"])
            pool.dma_start(mem[:, :, :], dram["memT"]).then_inc(mem_landed, 16)

        @block.tensor
        def _(pe):
            pe.wait_ge(first_landed, 16 * len(FIRST_CONSTS))
            tensor_linear_T(pe, b["sb_qkv"], 8, h_hi, h_lo, ready=ready("mix0"), root="mix0")
            tensor_linear_N(pe, b["sb_qkv"] + 8, 4, WHOLE)
            last = tensor_sb(pe)
            tensor_linear_T(pe, b["sb_o"], 4, o_hi, o_lo, ready=(blo_done, 1, 2), last=(7, last))
            tensor_mlp(pe, 0, "mlp0")
            tensor_linear_T(pe, b["kv"], 4, h_hi, h_lo, ready=ready("kv"), root="kv")
            tensor_block_N(pe, b["kv"] + 4, b["kv"] % 2, WHOLE)
            pe.wait_ge(tile_free, 4 + 2 * (b["kv"] + 4))
            tensor_rope(pe, 0, 2)
            tensor_block_N(pe, b["kv"] + 5, (b["kv"] + 1) % 2, WHOLE)
            tensor_rope(pe, 2, 2)
            tensor_compress(pe)

            def turn_queries(pair, then=None):
                def run(pe):
                    pe.wait_ge(tile_free, 4 + 2 * (b["q"] + pair + 1))
                    tensor_rope(pe, 4 + 2 * pair, 2)
                    if then is not None:
                        then(pe)
                return run
            tensor_linear_T(pe, b["q"], 4, h_hi, h_lo, ready=(r_ready, 0, 1), between={
                1: turn_queries(0), 2: turn_queries(1, tensor_turn_hidden), 3: turn_queries(2, tensor_compressed)})
            tensor_block_N(pe, b["gate"], b["gate"] % 2, GATES)
            turn_queries(3)(pe)
            pe.wait_ge(rope_ready, 6)
            pe.wait_ge(dup_k, 256)
            pe.wait_ge(ccmp_done, 2)
            pe.wait_ge(tile_free, 4 + 2 * b["nsa_o"])
            last = tensor_attention(pe, "nsa")
            tensor_linear_T(pe, b["nsa_o"], 4, o_hi, o_lo, ready=(olo_done, 1, 2), last=(7, last))
            tensor_mlp(pe, 1, "mlp1")
            def turn_tiles(first, n, blocks):
                def run(pe):
                    pe.wait_ge(tile_free, 4 + 2 * (b["in"] + blocks))
                    tensor_rope(pe, 4 + KT + first, n)
                return run
            tensor_linear_T(pe, b["in"], 6, h_hi, h_lo, ready=ready("mix2"), root="mix2", between={
                3: turn_tiles(0, 2, 3), 4: turn_tiles(2, 3, 4), 5: turn_tiles(5, 3, 5)})
            blk = b["in"] + 6
            tensor_block_T(pe, blk, blk % 2, h_hi, h_lo, S, tiles=(0,))
            tensor_block_N(pe, blk, blk % 2, VALUES_A)
            turn_tiles(8, 2, 6)(pe)
            tensor_block_N(pe, blk + 1, (blk + 1) % 2, WHOLE)
            turn_tiles(10, 3, 7)(pe)
            tensor_block_N(pe, blk + 2, blk % 2, WHOLE)
            pe.wait_ge(tile_free, 4 + 2 * b["out"])
            pe.wait_ge(rope_ready, 25)
            tensor_attention(pe, "diff")()
            pe.wait_ge(dup_a, 64)
            last = tensor_attention(pe, "swa")
            pe.wait_ge(dlo, 4)
            tensor_linear_T(pe, b["out"], 4, o_hi, o_lo, ready=(olo_done, ATT["swa"]["o0"] + 1, 2),
                            order=(4, 5, 6, 7, 0, 1, 2, 3), last=(3, last))
            tensor_linear_T(pe, b["ckv"], 4, m_hi, m_lo, tokens=MEM, ready=ready("cross"), root="cross")
            tensor_linear_N(pe, b["ckv"] + 4, 4, MEMORY)
            tensor_linear_T(pe, b["cq"], 4, h_hi, h_lo, ready=ready("cross", 1))
            pe.wait_ge(tile_free, 4 + 2 * b["co"])
            last = tensor_attention(pe, "cross")
            tensor_linear_T(pe, b["co"], 4, o_hi, o_lo, ready=lambda k: (olo_done, ATT["cross"]["o0"] + k // 2 + 1), last=(6, last))
            tensor_mlp(pe, 2, "mlp2")
            tensor_root(pe, "final2")

        @block.scalar
        def _(act):
            for name, t in FIRST_CONSTS:
                act.dma_start(full(t), dram[name]).then_inc(first_landed, 16)
            act.preload_act_table_set("natural_log_exp_and_others")
            scalar_split(act, 0, 0, 0)
            act.wait_ge(first_landed, 16 * len(FIRST_CONSTS))
            for t in range(KT):
                scalar_tile(act, "mix0", t, squares=False)
            scalar_linear(act, b["sb_qkv"], 12, root="mix0", between={2: scalar_consts})
            act.preload_act_table_set("natural_log_exp_and_others")
            scalar_sb(act)
            scalar_residual(act, "mlp0")
            scalar_mlp(act, 0, "mlp0", "kv")
            scalar_linear(act, b["kv"], 6, root="kv", between={4: scalar_rows(0), 5: scalar_rows(1)})
            scalar_compress(act)
            scalar_linear(act, b["q"], 4, between={1: scalar_gelu})
            scalar_gates(act)
            scalar_attention(act, "nsa")
            scalar_residual(act, "mlp1")
            scalar_mlp(act, 1, "mlp1", "mix2")
            scalar_linear(act, b["in"], 9, root="mix2", between={2: lambda act: scalar_trig(act, 0), 3: lambda act: scalar_trig(act, 1)})
            scalar_attention(act, "diff")
            scalar_attention(act, "swa")
            scalar_residual(act, "cross")
            scalar_linear(act, b["ckv"], 8, root="cross")
            scalar_linear(act, b["cq"], 4)
            scalar_attention(act, "cross")
            scalar_residual(act, "mlp2")
            scalar_mlp(act, 2, "mlp2", "final2")
            scalar_root(act, "final2")

        @block.vector
        def _(dve):
            for _ in range(4):
                dve.engine_nop().then_inc(tile_free, 1)
            vector_split(dve, 0, 0)
            dve.wait_ge(first_landed, 16 * len(FIRST_CONSTS))
            for t in range(KT):
                vector_tile(dve, "mix0", t, squares=False)
            vector_linear(dve, b["sb_qkv"], 8, to_T(dve, sb_qk), root="mix0", between={1: vector_consts})
            vector_linear(dve, b["sb_qkv"] + 8, 4, to_N(dve, sb_v))
            vector_sb(dve)
            vector_residual(dve, "mlp0")
            vector_mlp(dve, 0, "mlp0", "kv")
            vector_linear(dve, b["kv"], 4, to_T(dve, kv_nat), root="kv")
            vector_linear(dve, b["kv"] + 4, 1, to_N(dve, v_slc))
            vector_rows(0)(dve)
            vector_rope(dve, 0, 2)
            vector_linear(dve, b["kv"] + 5, 1, to_N(dve, v_win))
            vector_rows(1)(dve)
            vector_compress(dve)

            def behind_q0(dve):
                vector_rope(dve, 2, 2)
                vector_gelu_argument(dve)

            def behind_q1(dve):
                vector_gelu(dve)
                vector_rope(dve, 4, 2)

            def behind_q2(dve):
                vector_rope(dve, 6, 2)
                vector_turned(dve)

            def behind_q3(dve):
                dve.wait_ge(dup_k, 256)
                vector_rope(dve, 8, 2)
                vector_compressed(dve)
            vector_linear(dve, b["q"], 4, to_T(dve, q_plain),
                          between={0: behind_q0, 1: behind_q1, 2: behind_q2, 3: behind_q3})
            vector_gates(dve)
            vector_attention(dve, "nsa")
            vector_residual(dve, "mlp1")
            vector_mlp(dve, 1, "mlp1", "mix2")
            R = 4 + KT

            def first_turned(dve):
                dve.wait_ge(trig_a, 2)
                vector_rope(dve, R, 2)
            vector_linear(dve, b["in"], 6, to_T(dve, inp), root="mix2",
                          between={0: lambda dve: vector_place(dve, "final1", sq), 1: lambda dve: vector_trig(dve, 0),
                                   2: lambda dve: vector_trig(dve, 1), 3: first_turned, 4: lambda dve: vector_rope(dve, R + 2, 3),
                                   5: lambda dve: vector_rope(dve, R + 5, 3)})

            def ka_va(i, u, j, bank):
                if j == 0:
                    return dve.tensor_tensor(inp[:, 12, :], ps[:, bank, :], rstd[:, :], ALU.mult)
                return dve.tensor_tensor(va[:, :, :], ps[:, bank, :].rearrange("p (a b) -> p a b", a=QT),
                                         rcol[:, :].unsqueeze(2).broadcast_to([P, QT, P]), ALU.mult)
            vector_linear(dve, b["in"] + 6, 1, ka_va)
            vector_rope(dve, R + 8, 2)
            vector_linear(dve, b["in"] + 7, 2, to_N(dve, vd), between={0: lambda dve: vector_rope(dve, R + 10, 3)})
            vector_attention(dve, "diff")
            vector_attention(dve, "swa")
            dve.wait_ge(xn_ready, KT)
            vector_residual(dve, "cross")
            vector_linear(dve, b["ckv"], 4, to_T(dve, c_k, MEM, mrstd), root="cross")

            def memory_v(i, u, j, bank):
                return dve.tensor_scalar(c_v[:, j, span(BLK * (2 * i + u), BLK)], ps[:, bank, 0:BLK], rcol[:, j:j + 1], None, ALU.mult)
            vector_linear(dve, b["ckv"] + 4, 4, memory_v)
            vector_linear(dve, b["cq"], 4, to_T(dve, c_q))
            vector_attention(dve, "cross")
            vector_residual(dve, "mlp2")
            vector_mlp(dve, 2, "mlp2", "final2")
            vector_root(dve, "final2")
            vector_place(dve, "final2", rstd[:, :])


def weight_blocks(w):
    n = w.shape[1] // BLK
    return [np.ascontiguousarray(w[:, BLK * i:BLK * (i + 1)].reshape(KT, P, BLK).transpose(1, 0, 2)) for i in range(n)]


def mlp_blocks(w1, w2):
    out = []
    for c in range(CH):
        out += weight_blocks(w1[:, D * c:D * (c + 1)]) + weight_blocks(w2[D * c:D * (c + 1), :])
    return out


def features(a):
    return np.ascontiguousarray(a.T.reshape(-1, P, a.shape[0]).transpose(1, 0, 2))


def rotation(period, half):
    m = np.zeros((P, P), np.float32)
    for p in range(P):
        d = p % period
        if d < half:
            m[p + half, p] = -1.0
        elif d < 2 * half:
            m[p - half, p] = 1.0
    return m


def constants():
    f = np.float32
    q, k = np.arange(P)[:, None], np.arange(P)[None, :]
    c = {}
    c["m_sb"] = np.full((P, S), BIG, f)
    c["m_sb"][:, :P] = np.where(k > q, f(BIG), f(NEG))
    c["m_causal"] = np.zeros((P, S), f)
    c["m_causal"][:, S - P:] = np.where(k <= q, f(0), f(NEG))
    c["m_swa"] = np.zeros((P, 2 * P), f)
    c["m_swa"][:, :P] = np.where(k > q, f(0), f(NEG))
    c["m_swa"][:, P:] = np.where(k <= q, f(0), f(NEG))
    t = P * np.arange(QT)[None, :, None] + np.arange(P)[:, None, None]
    n = np.arange(NCP)[None, None, :]
    c["m_cmp"] = np.where((16 * n + 31 <= t) & (n < NCMP), f(0), f(NEG)).astype(f)
    c["anyv"] = (t[:, :, 0] >= 31).astype(f)
    c["ident"] = np.eye(P, dtype=f)
    c["ones"] = np.ones((P, P), f)
    c["upper"] = (q >= k).astype(f)
    c["rot1"] = rotation(HD, 8)
    c["rot2"] = rotation(HD, 32)
    inv = (f(500000.0) ** (-np.arange(8, dtype=f) * f(2.0) / f(16))).astype(f)
    ang = (np.arange(S, dtype=f)[None, :] * inv[:, None]).astype(f)
    c["cos1"], c["sin1"] = np.ones((P, S), f), np.zeros((P, S), f)
    for p in range(P):
        if p % HD < 16:
            c["cos1"][p], c["sin1"][p] = np.cos(ang[p % 8]), np.sin(ang[p % 8])
    inv2 = (f(10000.0) ** (-np.arange(0, HD, 2, dtype=f) / f(HD))).astype(f)
    c["invf"] = np.ascontiguousarray(inv2[np.arange(P) % 32][:, None])
    c["eps"] = np.tile(np.array([[EPS, EPS * EPS]], f), (P, 1))
    return c


def layout(i):
    blocks = weight_blocks(i["sb_w_qkv"][0]) + weight_blocks(i["sb_w_o"][0]) + mlp_blocks(i["mlp_w1"][0], i["mlp_w2"][0])
    kv = weight_blocks(i["nsa_w_kv"])
    blocks += [kv[0], kv[1], kv[2], kv[4], kv[3], kv[5]]
    for c in range(2):
        blocks += weight_blocks(i["cmp_w1"][c][:D]) + weight_blocks(i["cmp_w1"][c][D:])
    wq = i["nsa_w_q"][0]
    blocks += weight_blocks(wq[:, :D])
    blocks += weight_blocks(np.concatenate([wq[:, D:], np.zeros((D, BLK - 48), wq.dtype)], axis=1))
    blocks += weight_blocks(i["nsa_w_o"][0]) + mlp_blocks(i["mlp_w1"][1], i["mlp_w2"][1])
    win = weight_blocks(i["w_in_2"][0])
    blocks += [win[0], win[1], win[3], win[4], win[5], win[6], win[2], win[7], win[8]]
    blocks += weight_blocks(i["w_out_2"][0]) + weight_blocks(i["w_ckv_2"][0]) + weight_blocks(i["w_cq_2"][0])
    blocks += weight_blocks(i["w_co_2"][0]) + mlp_blocks(i["w_up_2"][0], i["w_down_2"][0])
    assert len(blocks) == NBLK
    gains = [i["norm_gain"][0, 0], i["norm_gain"][0, 1], i["kv_norm"], i["norm_gain"][1, 0], i["norm_gain"][1, 1], i["final_norm"],
             i["g_mix_2"][0], i["g_mem_2"][0], i["g_cross_2"][0], i["g_mlp_2"][0], i["g_final_2"]]
    rows = lambda a: np.ascontiguousarray(np.broadcast_to(a, (P,) + a.shape))
    lam = np.stack([i["lambda_q1_2"][0], i["lambda_k1_2"][0], i["lambda_q2_2"][0], i["lambda_k2_2"][0]])
    d = dict(
        wstream=np.stack(blocks), xT=features(i["x"][0]), memT=features(i["mem_2"][0]),
        gains=np.ascontiguousarray(np.stack(gains).reshape(len(GAINS), KT, P).transpose(2, 0, 1)),
        gate_b=rows(i["nsa_gate_b"][0]), sinks=rows(i["sinks_2"][0]), lamw=rows(lam),
        cpos=np.ascontiguousarray(i["cmp_pos"].reshape(2, 16, P).transpose(2, 0, 1)),
        w2c=np.ascontiguousarray(i["cmp_w2"].reshape(2, 2, P, HD).transpose(2, 0, 1, 3)),
        gdiff=np.ascontiguousarray(i["g_diff_2"][0][:, None]), positions=rows(i["positions_2"][0]))
    d.update(constants())
    return d


def kernel(**inputs):
    import concourse.bacc as bacc
    from concourse.bass_utils import run_bass_kernel_spmd

    arrays = layout({k: np.asarray(v) for k, v in inputs.items()})
    nc = bacc.Bacc("TRN2", target_bir_lowering=False, num_devices=1)
    dram = {n: nc.dram_tensor("in_" + n, a.shape, mybir.dt.from_np(a.dtype), kind="ExternalInput").ap() for n, a in arrays.items()}
    out = nc.dram_tensor("out_T", (P, KT, S), F32, kind="ExternalOutput").ap()
    build_program(nc, dram, out)
    r = run_bass_kernel_spmd(nc, [{"in_" + n: a for n, a in arrays.items()}], core_ids=[0])
    got = r.results[0]["out_T"]
    return np.ascontiguousarray(got.transpose(1, 0, 2).reshape(D, S).T)[None]
```
